# Optimizing a Trainium2 kernel written in Bass

```python
import jax, jax.numpy as jnp
from jax import lax
import numpy as np

D_MODEL = 2048
BATCH = 1
SEQ = 256
DEPTH = 1

LRU_WIDTH = 2560
LRU_HEADS = 20
LRU_HEAD_DIM = LRU_WIDTH // LRU_HEADS
LRU_CONV = 4
LRU_CONV_LEFT = 2
LRU_C = 8.0
CONV_WIDTH = 2048
CONV_GROUPS = 16
SHORT_CONV = 3
SHORT_CONV_LEFT = 1
D_FF = 4 * D_MODEL
ALPHA = float((2 * DEPTH) ** 0.25)
BETA = float((8 * DEPTH) ** -0.25)
LN_EPS = 1e-5
SPLIT_SIZES = (LRU_WIDTH, CONV_WIDTH, CONV_WIDTH, CONV_WIDTH, D_MODEL, D_MODEL)
SPLIT_POINTS = tuple(int(v) for v in np.cumsum(SPLIT_SIZES)[:-1])
IN_COLS = int(sum(SPLIT_SIZES))


def layer_norm(x, g, b):
    xf = x.astype(jnp.float32)
    mu = jnp.mean(xf, axis=-1, keepdims=True)
    var = jnp.mean(jnp.square(xf - mu), axis=-1, keepdims=True)
    y = (xf - mu) * lax.rsqrt(var + LN_EPS)
    return (y * g.astype(jnp.float32) + b.astype(jnp.float32)).astype(x.dtype)

def centred_dwconv(u, w, b, left):
    k_w = w.shape[0]
    s = u.shape[1]
    up = jnp.pad(u, ((0, 0), (left, k_w - 1 - left), (0, 0)))
    return sum(up[:, k:k + s] * w[k] for k in range(k_w)) + b

def _lin_combine(left, right):
    a1, b1 = left
    a2, b2 = right
    return a1 * a2, a2 * b1 + b2

def rg_lru_direction(u, w_a, b_a, w_x, b_x, lam, reverse):
    bsz, s, _ = u.shape
    uh = u.reshape(bsz, s, LRU_HEADS, LRU_HEAD_DIM)
    r = jax.nn.sigmoid(jnp.einsum('bshd,hde->bshe', uh, w_a) + b_a).reshape(bsz, s, LRU_WIDTH)
    i = jax.nn.sigmoid(jnp.einsum('bshd,hde->bshe', uh, w_x) + b_x).reshape(bsz, s, LRU_WIDTH)
    log_a = -LRU_C * r.astype(jnp.float32) * jax.nn.softplus(-lam.astype(jnp.float32))
    a = jnp.exp(log_a)
    gated_x = jnp.sqrt(-jnp.expm1(2.0 * log_a)) * (i * u).astype(jnp.float32)
    _, h = lax.associative_scan(_lin_combine, (a, gated_x), reverse=reverse, axis=1)
    return h.astype(u.dtype)

def first_inputs(seed: int = 0) -> dict:
    key = jax.random.key(seed)
    ks = jax.random.split(key, 24)
    f32 = jnp.float32
    nrm = lambda k, shape, scale: jax.random.normal(k, shape, f32) * scale
    x = jax.random.normal(ks[0], (BATCH, SEQ, D_MODEL), f32)
    w_in = nrm(ks[1], (D_MODEL, IN_COLS), D_MODEL ** -0.5)
    lru_conv_w = nrm(ks[2], (LRU_CONV, LRU_WIDTH), LRU_CONV ** -0.5)
    lru_conv_b = nrm(ks[3], (LRU_WIDTH,), 0.01)
    lru_w_a = nrm(ks[4], (2, LRU_HEADS, LRU_HEAD_DIM, LRU_HEAD_DIM), LRU_HEAD_DIM ** -0.5)
    lru_b_a = nrm(ks[5], (2, LRU_HEADS, LRU_HEAD_DIM), 0.01)
    lru_w_x = nrm(ks[6], (2, LRU_HEADS, LRU_HEAD_DIM, LRU_HEAD_DIM), LRU_HEAD_DIM ** -0.5)
    lru_b_x = nrm(ks[7], (2, LRU_HEADS, LRU_HEAD_DIM), 0.01)
    a_c = jax.random.uniform(ks[8], (2, LRU_WIDTH), f32, 0.9, 0.999)
    a0 = a_c ** (1.0 / LRU_C)
    lru_lambda = jnp.log(a0) - jnp.log1p(-a0)
    w_lru_out = nrm(ks[9], (LRU_WIDTH, D_MODEL), BETA * LRU_WIDTH ** -0.5)
    sc_conv_w = nrm(ks[10], (SHORT_CONV, CONV_WIDTH), SHORT_CONV ** -0.5)
    sc_conv_b = nrm(ks[11], (CONV_WIDTH,), 0.01)
    w_conv_out = nrm(ks[12], (CONV_WIDTH, D_MODEL), BETA * CONV_WIDTH ** -0.5)
    w_o = nrm(ks[13], (D_MODEL, D_MODEL), BETA * D_MODEL ** -0.5)
    ln1_g = 1.0 + nrm(ks[14], (D_MODEL,), 0.01)
    ln1_b = nrm(ks[15], (D_MODEL,), 0.01)
    mlp_w1 = nrm(ks[16], (D_MODEL, D_FF), D_MODEL ** -0.5)
    mlp_b1 = nrm(ks[17], (D_FF,), 0.01)
    mlp_w2 = nrm(ks[18], (D_FF, D_MODEL), BETA * D_FF ** -0.5)
    mlp_b2 = nrm(ks[19], (D_MODEL,), 0.01)
    ln2_g = 1.0 + nrm(ks[20], (D_MODEL,), 0.01)
    ln2_b = nrm(ks[21], (D_MODEL,), 0.01)
    return {"x": x, "w_in": w_in, "lru_conv_w": lru_conv_w, "lru_conv_b": lru_conv_b,
            "lru_w_a": lru_w_a, "lru_b_a": lru_b_a, "lru_w_x": lru_w_x, "lru_b_x": lru_b_x,
            "lru_lambda": lru_lambda, "w_lru_out": w_lru_out, "sc_conv_w": sc_conv_w,
            "sc_conv_b": sc_conv_b, "w_conv_out": w_conv_out, "w_o": w_o,
            "ln1_g": ln1_g, "ln1_b": ln1_b, "mlp_w1": mlp_w1, "mlp_b1": mlp_b1,
            "mlp_w2": mlp_w2, "mlp_b2": mlp_b2, "ln2_g": ln2_g, "ln2_b": ln2_b}

def first_block(x, w_in, lru_conv_w, lru_conv_b, lru_w_a, lru_b_a, lru_w_x, lru_b_x,
              lru_lambda, w_lru_out, sc_conv_w, sc_conv_b, w_conv_out, w_o,
              ln1_g, ln1_b, mlp_w1, mlp_b1, mlp_w2, mlp_b2, ln2_g, ln2_b):
    h = x
    for _ in range(DEPTH):
        proj = jnp.einsum('bsd,dc->bsc', h, w_in)
        lru_x, conv_x, conv_bg, conv_cg, g_lru, g_conv = jnp.split(proj, SPLIT_POINTS, axis=-1)
        u = centred_dwconv(lru_x, lru_conv_w, lru_conv_b, LRU_CONV_LEFT)
        h_fwd = rg_lru_direction(u, lru_w_a[0], lru_b_a[0], lru_w_x[0], lru_b_x[0], lru_lambda[0], False)
        h_bwd = rg_lru_direction(u, lru_w_a[1], lru_b_a[1], lru_w_x[1], lru_b_x[1], lru_lambda[1], True)
        y_lru = jnp.einsum('bsw,wd->bsd', h_fwd + h_bwd, w_lru_out)
        v = centred_dwconv(conv_cg * conv_x, sc_conv_w, sc_conv_b, SHORT_CONV_LEFT)
        y_conv = jnp.einsum('bsc,cd->bsd', conv_bg * v, w_conv_out)
        merged = jax.nn.sigmoid(g_lru) * y_lru + jax.nn.sigmoid(g_conv) * y_conv
        mix_out = jnp.einsum('bsd,de->bse', merged, w_o)
        h = layer_norm(ALPHA * h + mix_out, ln1_g, ln1_b)
        ff = jnp.square(jax.nn.relu(jnp.einsum('bsd,df->bsf', h, mlp_w1) + mlp_b1))
        ff_out = jnp.einsum('bsf,fd->bsd', ff, mlp_w2) + mlp_b2
        h = layer_norm(ALPHA * h + ff_out, ln2_g, ln2_b)
    return h


_first_inputs = first_inputs


def first_inputs(seed=0):
    import zlib

    import numpy as np

    out = dict(_first_inputs(seed))
    spreads = {}
    factors = {'lru_conv_b': 4.805,
     'lru_b_a': 193.568,
     'lru_b_x': 64.0,
     'sc_conv_b': 32.301,
     'ln1_g': 125.469,
     'ln1_b': 122.429,
     'mlp_b1': 127.441,
     'mlp_b2': 200.0,
     'ln2_g': 188.22,
     'ln2_b': 181.784}
    for name, (base, spread) in spreads.items():
        noise = np.random.default_rng([zlib.crc32(name.encode()), seed]).standard_normal(out[name].shape)
        drawn = base * np.exp(spread * noise) if base else spread * noise
        out[name] = __import__('jax').numpy.asarray(drawn.astype(out[name].dtype))
    for name, factor in factors.items():
        out[name] = (out[name] * factor).astype(out[name].dtype)
    return out


_narrow_inputs = first_inputs


def first_inputs(seed=0):

    out = dict(_narrow_inputs(seed))
    wider = {'ln1_g': 5.42, 'ln1_b': 5.42, 'mlp_b1': 5.42, 'mlp_b2': 12.0, 'ln2_g': 6.44, 'ln2_b': 6.44}
    for name, times in wider.items():
        mean = out[name].mean()
        out[name] = (mean + times * (out[name] - mean)).astype(out[name].dtype)
    return out


HEAD_DIM = 64
A_HEADS = 8
A_WIDTH = A_HEADS * HEAD_DIM
DILATED_PAIRS = ((128, 1), (512, 4), (2048, 16))
B_WIDTH = 512
CONV_WIDTH_2 = 31
C_Q_HEADS = 16
C_KV_HEADS = 2
C_WIDTH = C_Q_HEADS * HEAD_DIM
C_WINDOW = 128
MIX_WIDTH = A_WIDTH + B_WIDTH + C_WIDTH
IN_WIDTHS = (A_WIDTH, A_WIDTH, A_WIDTH,
             B_WIDTH, B_WIDTH,
             C_WIDTH, C_KV_HEADS * HEAD_DIM, C_KV_HEADS * HEAD_DIM)
IN_WIDTH = sum(IN_WIDTHS)
D_FF_2 = -(-(8 * D_MODEL) // (3 * 256)) * 256
BLOCK = 128
EPS = 1e-6


def _rms_norm(x, g):
    xf = x.astype(jnp.float32)
    y = xf * lax.rsqrt(jnp.mean(xf * xf, axis=-1, keepdims=True) + EPS)
    return (y * g.astype(jnp.float32)).astype(x.dtype)

def _layer_norm(x, g, b):
    xf = x.astype(jnp.float32)
    mu = jnp.mean(xf, axis=-1, keepdims=True)
    var = jnp.mean(jnp.square(xf - mu), axis=-1, keepdims=True)
    y = (xf - mu) * lax.rsqrt(var + EPS)
    return (y * g.astype(jnp.float32) + b.astype(jnp.float32)).astype(x.dtype)

def _band_attention(q, k, v, max_dist, sinks=None):
    N, L, Hq, hd = q.shape
    Hk = k.shape[2]
    G = Hq // Hk
    blk = min(BLOCK, L)
    nb = -(-L // blk)
    Lp = nb * blk
    C = blk + max_dist
    qb = jnp.pad(q, ((0, 0), (0, Lp - L), (0, 0), (0, 0))).reshape(N, nb, blk, Hk, G, hd)
    kp = jnp.pad(k, ((0, 0), (max_dist, Lp - L), (0, 0), (0, 0)))
    vp = jnp.pad(v, ((0, 0), (max_dist, Lp - L), (0, 0), (0, 0)))
    idx = jnp.arange(nb)[:, None] * blk + jnp.arange(C)[None, :]
    kb = kp[:, idx]
    vb = vp[:, idx]
    s = jnp.einsum('nbqhgd,nbkhd->nbhgqk', qb, kb,
                   preferred_element_type=jnp.float32) * (hd ** -0.5)
    qpos = jnp.arange(nb)[:, None] * blk + jnp.arange(blk)[None, :]
    kpos = idx - max_dist
    dist = qpos[:, :, None] - kpos[:, None, :]
    valid = (dist >= 0) & (dist <= max_dist) & (kpos[:, None, :] >= 0)
    s = jnp.where(valid[None, :, None, None], s, -jnp.inf)
    m = jnp.max(s, axis=-1)
    if sinks is not None:
        sk = sinks.astype(jnp.float32).reshape(Hk, G)[None, None, :, :, None]
        m = jnp.maximum(m, sk)
    p = jnp.exp(s - m[..., None])
    denom = jnp.sum(p, axis=-1)
    if sinks is not None:
        denom = denom + jnp.exp(sk - m)
    o = jnp.einsum('nbhgqk,nbkhd->nbqhgd', p, vb.astype(jnp.float32))
    denom_t = jnp.transpose(denom, (0, 1, 4, 2, 3))
    o = o / denom_t[..., None]
    lse = jnp.transpose(m, (0, 1, 4, 2, 3)) + jnp.log(denom_t)
    o = o.reshape(N, Lp, Hq, hd)[:, :L]
    lse = lse.reshape(N, Lp, Hq)[:, :L]
    return o, lse

def _dilated_mixture(q, k, v):
    B, S, H, hd = q.shape
    outs, lses = [], []
    for (w, d) in DILATED_PAIRS:
        def to_res(t):
            return t.reshape(B, S // d, d, H, hd).transpose(0, 2, 1, 3, 4).reshape(B * d, S // d, H, hd)
        o, lse = _band_attention(to_res(q), to_res(k), to_res(v), w // d)
        outs.append(o.reshape(B, d, S // d, H, hd).transpose(0, 2, 1, 3, 4).reshape(B, S, H, hd))
        lses.append(lse.reshape(B, d, S // d, H).transpose(0, 2, 1, 3).reshape(B, S, H))
    wts = jax.nn.softmax(jnp.stack(lses, axis=0), axis=0)
    return jnp.einsum('cbsh,cbshd->bshd', wts, jnp.stack(outs, axis=0))

def _conformer_conv(u, gate, conv_w, conv_b, ln_g, ln_b):
    h = u * jax.nn.sigmoid(gate)
    C = h.shape[-1]
    y = lax.conv_general_dilated(h, conv_w[:, None, :].astype(h.dtype), window_strides=(1,),
                                 padding=[(CONV_WIDTH_2 - 1, 0)],
                                 dimension_numbers=('NWC', 'WIO', 'NWC'),
                                 feature_group_count=C)
    y = y + conv_b
    return jax.nn.silu(_layer_norm(y, ln_g, ln_b))

def second_inputs(seed: int = 0) -> dict:
    key = jax.random.key(seed)
    ks = jax.random.split(key, 17)
    f32 = jnp.float32
    nrm = lambda k, shp: jax.random.normal(k, shp, dtype=f32)
    return {
        "x": nrm(ks[0], (BATCH, SEQ, D_MODEL)),
        "norm1_g": 1.0 + 0.02 * nrm(ks[1], (DEPTH, D_MODEL)),
        "w_in": nrm(ks[2], (DEPTH, D_MODEL, IN_WIDTH)) * D_MODEL ** -0.5,
        "a_q_g": 1.0 + 0.02 * nrm(ks[3], (DEPTH, HEAD_DIM)),
        "a_k_g": 1.0 + 0.02 * nrm(ks[4], (DEPTH, HEAD_DIM)),
        "conv_w": nrm(ks[5], (DEPTH, CONV_WIDTH_2, B_WIDTH)) * CONV_WIDTH_2 ** -0.5,
        "conv_b": 0.02 * nrm(ks[6], (DEPTH, B_WIDTH)),
        "conv_ln_g": 1.0 + 0.02 * nrm(ks[7], (DEPTH, B_WIDTH)),
        "conv_ln_b": 0.02 * nrm(ks[8], (DEPTH, B_WIDTH)),
        "c_q_g": 1.0 + 0.02 * nrm(ks[9], (DEPTH, HEAD_DIM)),
        "c_k_g": 1.0 + 0.02 * nrm(ks[10], (DEPTH, HEAD_DIM)),
        "c_sinks": 0.5 * nrm(ks[11], (DEPTH, C_Q_HEADS)),
        "w_out": nrm(ks[12], (DEPTH, MIX_WIDTH, D_MODEL)) * MIX_WIDTH ** -0.5,
        "norm2_g": 1.0 + 0.02 * nrm(ks[13], (DEPTH, D_MODEL)),
        "w_gate": nrm(ks[14], (DEPTH, D_MODEL, D_FF_2)) * D_MODEL ** -0.5,
        "w_up": nrm(ks[15], (DEPTH, D_MODEL, D_FF_2)) * D_MODEL ** -0.5,
        "w_down": nrm(ks[16], (DEPTH, D_FF_2, D_MODEL)) * D_FF_2 ** -0.5,
    }

def second_block(x, norm1_g, w_in, a_q_g, a_k_g, conv_w, conv_b, conv_ln_g, conv_ln_b,
              c_q_g, c_k_g, c_sinks, w_out, norm2_g, w_gate, w_up, w_down):
    B, S, _ = x.shape
    splits = [int(s) for s in np.cumsum(IN_WIDTHS)[:-1]]
    for l in range(DEPTH):
        h = _rms_norm(x, norm1_g[l])
        proj = h @ w_in[l]
        aq, ak, av, bu, bg, cq, ck, cv = jnp.split(proj, splits, axis=-1)
        aq = _rms_norm(aq.reshape(B, S, A_HEADS, HEAD_DIM), a_q_g[l])
        ak = _rms_norm(ak.reshape(B, S, A_HEADS, HEAD_DIM), a_k_g[l])
        av = av.reshape(B, S, A_HEADS, HEAD_DIM)
        out_a = _dilated_mixture(aq, ak, av).reshape(B, S, A_WIDTH)
        out_b = _conformer_conv(bu, bg, conv_w[l], conv_b[l], conv_ln_g[l], conv_ln_b[l])
        cq = _rms_norm(cq.reshape(B, S, C_Q_HEADS, HEAD_DIM), c_q_g[l])
        ck = _rms_norm(ck.reshape(B, S, C_KV_HEADS, HEAD_DIM), c_k_g[l])
        cv = cv.reshape(B, S, C_KV_HEADS, HEAD_DIM)
        out_c, _ = _band_attention(cq, ck, cv, C_WINDOW - 1, sinks=c_sinks[l])
        out_c = out_c.reshape(B, S, C_WIDTH)
        mix = jnp.concatenate([out_a.astype(x.dtype), out_b.astype(x.dtype),
                               out_c.astype(x.dtype)], axis=-1)
        x = x + mix @ w_out[l]
        h2 = _rms_norm(x, norm2_g[l])
        x = x + (jax.nn.silu(h2 @ w_gate[l]) * (h2 @ w_up[l])) @ w_down[l]
    return x


def setup_inputs(seed=0):
    out = dict(first_inputs(seed))
    for name, value in second_inputs(seed + 1).items():
        if name != "x":
            out[name + "_2"] = value
    return out


def reference(
    x, w_in, lru_conv_w, lru_conv_b, lru_w_a, lru_b_a, lru_w_x, lru_b_x, lru_lambda, w_lru_out,
    sc_conv_w, sc_conv_b, w_conv_out, w_o, ln1_g, ln1_b, mlp_w1, mlp_b1, mlp_w2, mlp_b2, ln2_g,
    ln2_b, norm1_g_2, w_in_2, a_q_g_2, a_k_g_2, conv_w_2, conv_b_2, conv_ln_g_2, conv_ln_b_2,
    c_q_g_2, c_k_g_2, c_sinks_2, w_out_2, norm2_g_2, w_gate_2, w_up_2, w_down_2,
):
    x = first_block(
        x, w_in, lru_conv_w, lru_conv_b, lru_w_a, lru_b_a, lru_w_x, lru_b_x, lru_lambda,
        w_lru_out, sc_conv_w, sc_conv_b, w_conv_out, w_o, ln1_g, ln1_b, mlp_w1, mlp_b1, mlp_w2,
        mlp_b2, ln2_g, ln2_b,
    )
    return second_block(
        x, norm1_g_2, w_in_2, a_q_g_2, a_k_g_2, conv_w_2, conv_b_2, conv_ln_g_2, conv_ln_b_2,
        c_q_g_2, c_k_g_2, c_sinks_2, w_out_2, norm2_g_2, w_gate_2, w_up_2, w_down_2,
    )


_drawn_inputs = setup_inputs


def setup_inputs(seed=0):
    import zlib

    import numpy as np

    out = dict(_drawn_inputs(seed))
    spreads = {}
    factors = {'mlp_b2': 8.0,
     'norm1_g_2': 8.0,
     'w_in_2': 8.0,
     'a_q_g_2': 8.0,
     'a_k_g_2': 8.0,
     'conv_w_2': 8.0,
     'conv_b_2': 200.0,
     'conv_ln_g_2': 200.0,
     'conv_ln_b_2': 200.0,
     'c_q_g_2': 8.0,
     'c_k_g_2': 8.0,
     'c_sinks_2': 21.434,
     'w_out_2': 8.0,
     'norm2_g_2': 8.0,
     'w_gate_2': 8.0,
     'w_up_2': 8.0,
     'w_down_2': 8.0}
    for name, (base, spread) in spreads.items():
        noise = np.random.default_rng([zlib.crc32(name.encode()), seed]).standard_normal(out[name].shape)
        drawn = base * np.exp(spread * noise) if base else spread * noise
        out[name] = __import__('jax').numpy.asarray(drawn.astype(out[name].dtype))
    for name, factor in factors.items():
        out[name] = (out[name] * factor).astype(out[name].dtype)
    return out
```

```python
from contextlib import ExitStack

import numpy as np
import concourse.bass as bass
from concourse import mybir

P = 128
S = 256
D = 2048
LRU_W, LRU_HEADS = 2560, 20
CONV_W = 2048
D_FF = 4 * D
D_FF2 = 5632
A_HEADS, C_HEADS, C_KV, HD = 8, 16, 2, 64
TAPS2 = 31
ALPHA = float(2 ** 0.25)
LN_EPS, RMS_EPS = 1e-5, 1e-6
KT = D // P
HT = LRU_W // P
SN = 4
N8, N10 = 8 * P, 10 * P
RING = 4
LRU_C = 8.0

ALU = mybir.AluOpType
ACT = mybir.ActivationFunctionType
AX = mybir.AxisListType
F32 = mybir.dt.float32
F32R = mybir.dt.float32r

PARAM_SIZES = [
    ("lru_w", 4 * HT), ("lru_b", HT), ("b_a", 2 * HT), ("b_x", 2 * HT), ("lam", 2 * HT),
    ("sc_w", 3 * KT), ("sc_b", KT), ("ln1_g", KT), ("ln1_b", KT), ("b1", D_FF // P), ("b2", KT),
    ("ln2_g", KT), ("ln2_b", KT), ("n1_g", KT), ("aq_g", 1), ("ak_g", 1), ("cq_g", 1), ("ck_g", 1),
    ("cv_w", 4 * TAPS2), ("cv_b", 4), ("cln_g", 4), ("cln_b", 4), ("n2_g", KT), ("sinks", C_HEADS),
]
COL = {}
_at = 0
for _name, _n in PARAM_SIZES:
    COL[_name] = _at
    _at += _n
NPARAM = _at
NCONST = P + 2 * 3 * P + 2


class Steps:

    def __init__(self, eng, sem):
        self.eng, self.sem, self.base, self.n = eng, sem, 0, 0

    def done(self, ins):
        ins.then_inc(self.sem, 1)
        self.n += 1
        return self.n

    def need(self, n=None):
        self.eng.wait_ge(self.sem, self.base + (self.n if n is None else n))

    def enter(self, i, per):
        self.before, self.per = self.base + self.n, per
        self.base, self.n = self.before + i * per, 0

    def leave(self, times):
        assert self.n == self.per, (self.n, self.per)
        self.base, self.n = self.before + times * self.per, 0


def ds(a, n):
    return slice(a, a + n) if isinstance(a, int) else bass.ds(a, n)


def build(nc, x_in, prm_in, const_in, w8, w10, out):
    with ExitStack() as ctx:
        def sb(name, shape, dt=F32, where=ctx):
            return where.enter_context(nc.sbuf_tensor(name, shape, dt))

        def sem(name):
            return ctx.enter_context(nc.semaphore(name))

        w_raw = sb("w_raw", [P, RING, N10])
        w_hi = sb("w_hi", [P, RING, N10], F32R)
        w_lo = sb("w_lo", [P, RING, N10], F32R)
        xx = sb("xx", [P, KT, 2 * S], F32R)
        half = sb("half", [P, SN, S])
        prm = sb("prm", [P, NPARAM])
        const = sb("const", [P, NCONST])
        ident, masks = const[:, 0:P], const[:, P:P + 768].rearrange("p (m n) -> p m n", m=2)
        pair_ones = const[:, 896:898]
        ones = sb("ones", [P, P])
        eps = sb("eps", [P, 2])
        decay = sb("decay", [P, 2 * HT])
        series = sb("series", [P, 3, 2 * HT])
        padded = sb("padded", [P, SN, S + 4])

        def region(*tensors):
            with ExitStack() as stack:
                return [sb(n, shape, dt, stack) for n, shape, dt in tensors]

        def in_turn(name, size, *phases):
            made = [region(*tensors) for tensors in phases]
            sb(name, [P, size])
            return made

        (hh,), (mx,), (res, bconv, probs, probs_t, vt) = in_turn(
            "region_h", HT * 2 * S,
            [("hh", [P, HT, 2 * S], F32R)],
            [("mx", [P, KT, 2 * S], F32R)],
            [("res", [P, KT, S], F32),
             ("bconv", [P, 4, S], F32),
             ("probs", [P, 2, 2, 3 * P], F32),
             ("probs_t", [P, 2, 2, 3 * P], F32),
             ("vt", [P, 2, 5, P], F32)])
        (gates,), (v32,), (m32,), (squares,), (rn_rows,), (ff,) = in_turn(
            "region_g", KT * S,
            [("gates", [P, SN, 2, 2, S], F32)],
            [("v32", [P, KT, S], F32)],
            [("m32", [P, KT, S], F32)],
            [("squares", [P, KT, S], F32)],
            [("rn_rows", [P, 2, 5, P], F32)],
            [("ff", [P, 8, 2 * S], F32R)])
        (la, aa, tt, uu), (vv,), (zz, mean, rstd, sdev, hnorm), (qkv,) = in_turn(
            "region_v", KT * 2 * S,
            [("la", [P, 2, SN, S], F32),
             ("aa", [P, 2, SN, S], F32),
             ("tt", [P, 2, SN, S], F32),
             ("uu", [P, SN, 2 * S], F32R)],
            [("vv", [P, KT, 2 * S], F32R)],
            [("zz", [P, KT, S], F32), ("mean", [P, S], F32), ("rstd", [P, S], F32),
             ("sdev", [P, S], F32), ("hnorm", [P, 2, SN, S], F32)],
            [("qkv", [P, 30, S], F32)])
        (uf,), (hid,), (bpad,), (bsq, sq_last, bmean, bsdev) = in_turn(
            "region_u", 2 * SN * S,
            [("uf", [P, 2, SN, S], F32)],
            [("hid", [P, 2, SN, S], F32)],
            [("bpad", [P, 4, S + 32], F32)],
            [("bsq", [P, 4, S], F32), ("sq_last", [P, S], F32), ("bmean", [P, S], F32), ("bsdev", [P, S], F32)])
        ssd = sb("ssd", [P, 2, 17, 2])
        rn = sb("rn", [P, 2, 17, 2])
        rq = sb("rq", [P, 2, 17, 2])
        gqk = sb("gqk", [P, 2])
        peak = sb("peak", [P, 2, 2, 2])
        negm = sb("negm", [P, 2, 2, 2])
        rsum = sb("rsum", [P, 2, 2, 2])
        sink = sb("sink", [P, 2, 2, 2])

        GA = ctx.enter_context(nc.psum_tensor("ps_a", [P, SN, 512], F32))
        GB = ctx.enter_context(nc.psum_tensor("ps_b", [P, SN, 512], F32))
        psum = (GA, GB)

        raw_in = [sem(f"raw_in{r}") for r in range(RING)]
        hi_done = sem("hi_done")
        lo_vec = sem("lo_vec")
        lo_pool = sem("lo_pool")
        pe_piece = sem("pe_piece")
        half_out = sem("half_out")
        strip_out = sem("strip_out")
        dve_step, pool_step = sem("dve_step"), sem("pool_step")
        params_in, const_in_sem = sem("params_in"), sem("const_in_sem")
        x_loaded = [sem(f"x_in{b}") for b in range(4)]
        const_ready = sem("const_ready")
        exp_lam = sem("exp_lam")
        xx_hi, xx_lo = sem("xx_hi"), sem("xx_lo")
        u_made, u_hi, u_lo = sem("u_made"), sem("u_hi"), sem("u_lo")
        gate_psum, gate_out = sem("gate_psum"), sem("gate_out")
        la_ready, iu_ready, a_ready, sq_ready = sem("la_ready"), sem("iu_ready"), sem("a_ready"), sem("sq_ready")
        tanh_ready, one_minus, root_ready = sem("tanh_ready"), sem("one_minus"), sem("root_ready")
        h_sum, h_hi, h_lo = sem("h_sum"), sem("h_hi"), sem("h_lo")
        vg_made, vg_hi, vg_lo = sem("vg_made"), sem("vg_hi"), sem("vg_lo")
        gl_sig = sem("gl_sig")
        m_made, m_hi, m_lo = sem("m_made"), sem("m_hi"), sem("m_lo")
        z_made = sem("z_made")
        ff_made, ff_hi, ff_lo, res_seed = sem("ff_made"), sem("ff_hi"), sem("ff_lo"), sem("res_seed")
        nsum, nmean, ncent, nsq, nvar, nsd, nh = (
            [sem(f"{k}{n}") for n in range(4)]
            for k in ("norm_sum", "norm_mean", "norm_centred", "norm_sq", "norm_var", "norm_sd", "norm_h"))
        bg_sum, bg_sig, b_made = sem("bg_sum"), sem("bg_sig"), sem("b_made")
        b_sum, b_mean, b_cent, b_sq, b_var, b_sd, b_norm, b_silu = (
            sem(n) for n in ("b_sum", "b_mean", "b_cent", "b_sq", "b_var", "b_sd", "b_norm", "b_silu"))
        qk_sq, qk_ssq, qk_sd, qk_rn, rows_ready, k_rows, k_ready = (
            sem(n) for n in ("qk_sq", "qk_ssq", "qk_sd", "qk_rn", "rows_ready", "k_rows", "k_ready"))
        vt_psum, vt_out = sem("vt_psum"), sem("vt_out")
        score_psum, score_out, peak_ready, exp_done, sink_done, rsum_ready, p_ready = (
            sem(n) for n in ("score_psum", "score_out", "peak_ready", "exp_done", "sink_done", "rsum_ready", "p_ready"))
        pt_psum, pt_out, o_psum = sem("pt_psum"), sem("pt_out"), sem("o_psum")
        gate_sum, gate_act, up_made = sem("gate_sum"), sem("gate_act"), sem("up_made")
        out_done = sem("out_done")

        XX_X, XX_H1, XX_N1, XX_MIX, XX_N2 = range(5)
        PAIRS = [(8 + t, 12 + t, t, 0) for t in range(4)] + [(20 + t, 28, 4, 1) for t in range(8)]
        NORMED = list(range(8, 16)) + list(range(20, 29))
        block = ctx.enter_context(nc.Block())

        @block.sync
        def _(sp):
            for b in range(4):
                sp.dma_start(zz[:, 4 * b:4 * b + 4, :], x_in[:, 4 * b:4 * b + 4, :]).then_inc(x_loaded[b], 16)

            def quad(q, src, at, width):
                for r in range(RING):
                    if not (isinstance(q, int) and q == 0):
                        sp.wait_ge(lo_vec if r % 2 == 0 else lo_pool, 2 * q - 1 + r // 2)
                    sp.dma_start(w_raw[:, r, 0:width], src[ds(at + r, 1), :, :].rearrange("a p n -> (a p) n")
                                 ).then_inc(raw_in[r], 16)

            quad(0, w8, 0, N8)
            sp.dma_start(prm[:, :], prm_in).then_inc(params_in, 16)
            sp.dma_start(const[:, :], const_in).then_inc(const_in_sem, 16)
            quad(1, w8, 4, N8)
            with sp.Fori(0, 10) as i:
                quad(i + 2, w10, 4 * i, N10)
            with sp.Fori(0, 22) as i:
                quad(i + 12, w8, 4 * i + 8, N8)
            with sp.Fori(0, 4) as i:
                for k in range(2):
                    quad(8 * i + 34 + k, w8, 24 * i + 96 + 4 * k, N8)
                for k in range(2):
                    quad(8 * i + 36 + k, w10, 8 * i + 40 + 4 * k, N10)
                for k in range(4):
                    quad(8 * i + 38 + k, w8, 24 * i + 104 + 4 * k, N8)
            with sp.Fori(0, 161) as i:
                quad(i + 66, w8, 4 * i + 192, N8)
            for j in range(4):
                sp.wait_ge(strip_out, 160 + j)
                sp.dma_start(out[:, 4 * j:4 * j + 4, :], res[:, 4 * j:4 * j + 4, :]).then_inc(out_done, 16)
            sp.wait_ge(out_done, 64)

        @block.tensor
        def _(pe):
            def piece_ready(q, r):
                pe.wait_ge(hi_done, 4 * q + r + 1)
                pe.wait_ge(lo_vec if r % 2 == 0 else lo_pool, 2 * q + 1 + r // 2)

            def strip(q, e, group, src, kt, need, per=8, gates_of=None, nout=SN, free=None, r0=0):
                tiles = [(k, j) for k in range(kt) for j in range(nout)]
                if gates_of is not None:
                    tiles += [(None, n) for n in range(16)]
                free()
                for first in range(0, len(tiles), per):
                    g = first // per + r0
                    r = g % 4
                    piece_ready(q + g // 4, r)
                    for o, (k, j) in enumerate(tiles[first:first + per]):
                        cols = slice(o * P, o * P + P)
                        if k is None:
                            last = gate_product(gates_of, j, r, cols)
                            continue
                        if j == 0:
                            need(k)
                        nc.tensor.matmul(group[:, j, :], w_hi[:, r, cols], src[:, k, :], start=k == 0, stop=False)
                        last = nc.tensor.matmul(group[:, j, 0:S], w_lo[:, r, cols], src[:, k, 0:S],
                                                start=False, stop=k == kt - 1)
                    last.then_inc(pe_piece, 1)

            def gate_product(s, n, r, cols):
                if n == 0:
                    pe.wait_ge(u_hi, s)
                    pe.wait_ge(u_lo, s)
                if n % 2 == 0:
                    pe.wait_ge(gate_out, 8 * (s - 1) + n // 2 + 1)
                dst = GB[:, (n // 2) % 4, (n % 2) * S:(n % 2) * S + S]
                hd = n // 4
                nc.tensor.matmul(dst, w_hi[:, r, cols], uu[:, hd, 0:S], start=True, stop=False)
                nc.tensor.matmul(dst, w_hi[:, r, cols], uu[:, hd, S:2 * S], start=False, stop=False)
                last = nc.tensor.matmul(dst, w_lo[:, r, cols], uu[:, hd, 0:S], start=False, stop=True)
                if n % 2 == 1 and n not in (5, 15):
                    last.then_inc(gate_psum, 1)
                return last

            def need_x(version):
                def need(k):
                    if k % 4 == 0:
                        pe.wait_ge(xx_hi, 4 * version + k // 4 + 1)
                        pe.wait_ge(xx_lo, 4 * version + k // 4 + 1)
                return need

            def nothing(k):
                pass

            def out_before(e):
                return lambda: pe.wait_ge(strip_out, e - 1)

            strip(0, 0, GA, xx, KT, need_x(XX_X), free=lambda: None)
            with pe.Fori(0, 2) as i:
                for k in range(2):
                    s = 2 * i + 1 + k
                    strip(2 * s, s, GA, xx, KT, nothing, per=10, gates_of=s, free=lambda: pe.wait_ge(strip_out, s))
            strip(10, 5, GA, xx, KT, nothing, per=10, gates_of=5, free=lambda: pe.wait_ge(strip_out, 5))
            strip(12, 6, GB, xx, KT, nothing, free=lambda: pe.wait_ge(gate_out, 44))
            with pe.Fori(0, 3) as i:
                strip(4 * i + 14, 2 * i + 7, GA, xx, KT, nothing, free=out_before(2 * i + 7))
                strip(4 * i + 16, 2 * i + 8, GB, xx, KT, nothing, free=out_before(2 * i + 8))
            with pe.Fori(0, 2) as i:
                strip(4 * i + 26, 2 * i + 13, GA, xx, KT, nothing, free=out_before(2 * i + 13))
                strip(4 * i + 28, 2 * i + 14, GB, xx, KT, nothing, free=out_before(2 * i + 14))
            def need_h(k):
                if k == 0:
                    pe.wait_ge(h_hi, 5)
                    pe.wait_ge(h_lo, 5)

            def need_v(k):
                if k % 4 == 0:
                    pe.wait_ge(vg_hi, k // 4 + 1)
                    pe.wait_ge(vg_lo, k // 4 + 1)

            with pe.Fori(0, 4) as i:
                q, e = 8 * i + 34, 4 * i + 17
                strip(q, e, GA, xx, KT, nothing, free=out_before(e))
                strip(q + 2, e + 1, GB, hh, HT, need_h, per=10, free=out_before(e + 1))
                strip(q + 4, e + 2, GA, xx, KT, nothing, free=out_before(e + 2))
                strip(q + 6, e + 3, GB, vv, KT, need_v, free=out_before(e + 3))

            def need_m(k):
                if k % 4 == 0:
                    pe.wait_ge(m_hi, k // 4 + 1)
                    pe.wait_ge(m_lo, k // 4 + 1)

            with pe.Fori(0, 2) as i:
                strip(4 * i + 66, 2 * i + 33, GA, mx, KT, need_m, free=out_before(2 * i + 33))
                strip(4 * i + 68, 2 * i + 34, GB, mx, KT, need_m, free=out_before(2 * i + 34))

            def column_sums(src, ready, done, bank, tiles=KT):
                for k in range(tiles):
                    if k % 4 == 0:
                        ready(k // 4)
                    last = nc.tensor.matmul(bank, ones[:, :], src[:, k, :], start=k == 0, stop=k == tiles - 1)
                last.then_inc(done, 1)

            pe.wait_ge(const_ready, 1)
            pe.wait_ge(strip_out, 36)
            column_sums(zz, lambda b: pe.wait_ge(z_made, b + 1), nsum[0], GA[:, 0, 0:S])
            column_sums(squares, lambda b: pe.wait_ge(nsq[0], b + 1), nvar[0], GA[:, 1, 0:S])

            def need_ff(before):
                def need(k):
                    if k % 4 == 0:
                        pe.wait_ge(ff_hi, before + k // 4 + 1)
                        pe.wait_ge(ff_lo, before + k // 4 + 1)
                return need

            with pe.Fori(0, 8) as i:
                q, e = 8 * i + 74, 6 * i + 37
                strip(q, e, GA, xx, KT, need_x(XX_H1), free=out_before(e))
                strip(q + 2, e + 1, GB, xx, KT, nothing, free=out_before(e + 1))
                for j in range(4):
                    strip(q + 4 + j, e + 2 + j, psum[j % 2], ff, 8, need_ff(2 * i), free=out_before(e + 2 + j))
            pe.wait_ge(strip_out, 84)
            column_sums(res, lambda b: pe.wait_ge(strip_out, 82 + b), nsum[1], GA[:, 0, 0:S])
            column_sums(squares, lambda b: pe.wait_ge(nsq[1], b + 1), nvar[1], GA[:, 1, 0:S])
            column_sums(squares, lambda b: pe.wait_ge(nsq[2], b + 1), nvar[2], GA[:, 1, 0:S])
            strip(138, 85, GA, xx, KT, need_x(XX_N1), free=out_before(85))
            strip(140, 86, GB, xx, KT, nothing, free=out_before(86))
            with pe.Fori(0, 2) as i:
                strip(4 * i + 142, 2 * i + 87, GA, xx, KT, nothing, free=out_before(2 * i + 87))
                strip(4 * i + 144, 2 * i + 88, GB, xx, KT, nothing, free=out_before(2 * i + 88))
            strip(150, 91, GA, xx, KT, nothing, free=out_before(91))
            strip(152, 92, GB, xx, KT, nothing, nout=2, free=out_before(92))
            pe.wait_ge(const_in_sem, 16)
            pe.wait_ge(strip_out, 93)
            column_sums(bconv, lambda b: pe.wait_ge(b_made, 4), b_sum, GA[:, 3, 0:S], 4)
            for n, tile in enumerate(NORMED):
                if n in (0, 8, 16):
                    pe.wait_ge(qk_sq, n // 8 + 1)
                src = sq_last if n == 16 else squares[:, n, :]
                for blk in range(2):
                    last = nc.tensor.matmul(GB[:, 3, (blk * 17 + n) * 2:(blk * 17 + n) * 2 + 2],
                                            src[:, blk * P:blk * P + P], pair_ones, start=True, stop=True)
            last.then_inc(qk_ssq, 1)
            for n in range(5):
                tile = 16 + n if n < 4 else 29
                for blk in range(2):
                    m = blk * 5 + n
                    last = nc.tensor.transpose(GA[:, m // 4, (m % 4) * P:(m % 4) * P + P],
                                               qkv[:, tile, blk * P:blk * P + P], ident)
            last.then_inc(vt_psum, 1)
            column_sums(bsq, lambda b: pe.wait_ge(b_sq, 1), b_var, GA[:, 3, S:2 * S], 4)
            pe.wait_ge(rows_ready, 1)
            for n in range(5):
                for blk in range(2):
                    last = nc.tensor.matmul(GB[:, n // 2, (n % 2) * S + blk * P:(n % 2) * S + blk * P + P],
                                            rn_rows[:, blk, n, :], ident, start=True, stop=True)
            last.then_inc(k_rows, 1)

            def scores(n):
                qt, kt_, _, _ = PAIRS[n]
                if n == 0:
                    pe.wait_ge(vt_out, 1)
                    pe.wait_ge(b_sd, 1)
                    pe.wait_ge(k_ready, 1)
                if n >= 2:
                    pe.wait_ge(score_out, n - 1)
                for hd in range(2):
                    part = slice(64 * hd, 64 * hd + 64)
                    bank = GA[:, 2 * (n % 2) + hd, :]
                    nc.tensor.matmul(bank[:, 0:P], qkv[part, qt, 0:P], qkv[part, kt_, 0:P], start=True, stop=True)
                    last = nc.tensor.matmul(bank[:, P:3 * P], qkv[part, qt, P:S], qkv[part, kt_, 0:S],
                                            start=True, stop=True)
                last.then_inc(score_psum, 1)

            def transposes(n):
                pe.wait_ge(p_ready, n + 1)
                if n >= 1:
                    pe.wait_ge(pt_out, n)
                for hd in range(2):
                    for c in range(3):
                        cols = slice(c * P, c * P + P)
                        last = nc.tensor.transpose(GB[:, hd, cols], probs[:, n % 2, hd, cols], ident)
                last.then_inc(pt_psum, 1)

            def values(n):
                v = PAIRS[n][2]
                pe.wait_ge(pt_out, n + 1)
                if n >= 2:
                    pe.wait_ge(xx_lo, 12 + 1 + n - 1)
                for hd in range(2):
                    part = slice(64 * hd, 64 * hd + 64)
                    bank = GB[part, 2 + n % 2, :]
                    nc.tensor.matmul(bank[:, 0:S], vt[:, 0, v, part], probs_t[:, n % 2, hd, 0:S], start=True, stop=False)
                    last = nc.tensor.matmul(bank[:, P:S], vt[:, 1, v, part], probs_t[:, n % 2, hd, 2 * P:3 * P],
                                            start=False, stop=True)
                last.then_inc(o_psum, 1)

            scores(0)
            for n in range(12):
                if n < 11:
                    scores(n + 1)
                if n >= 1:
                    values(n - 1)
                transposes(n)
            values(11)
            def need_mix(k):
                if k == 0:
                    pe.wait_ge(xx_hi, 25)
                    pe.wait_ge(xx_lo, 25)

            with pe.Fori(0, 2) as i:
                strip(4 * i + 153, 2 * i + 93, GA, xx, KT, need_mix, free=out_before(2 * i + 93))
                strip(4 * i + 155, 2 * i + 94, GB, xx, KT, nothing, free=out_before(2 * i + 94))
            pe.wait_ge(strip_out, 96)
            column_sums(squares, lambda b: pe.wait_ge(nsq[3], b + 1), nvar[3], GA[:, 1, 0:S])

            def need_n2(k):
                if k % 4 == 0:
                    pe.wait_ge(xx_hi, 25 + k // 4 + 1)
                    pe.wait_ge(xx_lo, 25 + k // 4 + 1)

            def down(q, e, n):
                for j in range(4):
                    strip(q + j // 2, e + j, psum[(j + 1) % 2], ff, 4, need_ff(n + 15), free=out_before(e + j),
                          r0=2 * (j % 2))

            strip(161, 97, GA, xx, KT, need_n2, free=out_before(97))
            strip(163, 98, GB, xx, KT, nothing, free=out_before(98))
            with pe.Fori(0, 10) as i:
                q, e = 6 * i + 165, 6 * i + 99
                strip(q, e, GA, xx, KT, nothing, free=out_before(e))
                down(q + 2, e + 1, i + 1)
                strip(q + 4, e + 5, GB, xx, KT, nothing, free=out_before(e + 5))
            for j in range(4):
                strip(225 + j // 2, 159 + j, psum[j % 2], ff, 4, need_ff(26), free=out_before(159 + j), r0=2 * (j % 2))

        @block.scalar
        def _(act):
            def split(q, r, width=N8):
                act.wait_ge(raw_in[r], 16 * q + 16)
                if not (isinstance(q, int) and q == 0):
                    act.wait_ge(pe_piece, 4 * q + r - 3)
                act.activation(w_hi[:, r, 0:width], w_raw[:, r, 0:width], ACT.Copy).then_inc(hi_done, 1)

            def splits(q, width=N8, slots=range(RING)):
                for r in slots:
                    split(q, r, width)

            def halves(e, pieces, group, nout=SN):
                act.wait_ge(pe_piece, pieces)
                if not (isinstance(e, int) and e == 0):
                    act.wait_ge(strip_out, e)
                act.activation(half[:, 0:nout, :], group[:, 0:nout, S:2 * S], ACT.Copy).then_inc(half_out, 1)

            def hi_of(dst, src, made, n, done):
                act.wait_ge(made, n)
                act.activation(dst, src, ACT.Copy).then_inc(done, 1)

            splits(0)
            for b in range(4):
                act.wait_ge(x_loaded[b], 16)
                act.activation(xx[:, 4 * b:4 * b + 4, 0:S], zz[:, 4 * b:4 * b + 4, :], ACT.Copy).then_inc(xx_hi, 1)
            act.wait_ge(const_ready, 2)
            act.activation(decay[:, :], decay[:, :], ACT.Exp, scale=-1.0).then_inc(exp_lam, 1)
            splits(1)
            splits(2, N10)
            halves(0, 8, GA)
            hi_of(uu[:, :, 0:S], uf[:, 0, :, :], u_made, 1, u_hi)

            def gates_out(s, banks):
                for n in banks:
                    hd, way = n // 2, n % 2
                    if n in (2, 7):
                        act.wait_ge(pe_piece, 8 * s + (7 if n == 2 else 8))
                    else:
                        act.wait_ge(gate_psum, 6 * (s - 1) + (n if n < 2 else n - 1) + 1)
                    for kind, name in enumerate(("b_a", "b_x")):
                        last = act.activation(gates[:, hd, way, kind, :], GB[:, n % 4, kind * S:kind * S + S],
                                              ACT.Sigmoid, bias=prm[:, ds(COL[name] + way * HT + hd - 4 + 4 * s, 1)])
                    last.then_inc(gate_out, 1)

            def lru_strip(s, width_next, conv):
                q = 2 * s
                splits(q + 1, N10)
                splits(q + 2, width_next, (0, 1))
                act.wait_ge(h_sum, s)
                gates_out(s, range(0, 3))
                split(q + 2, 2, width_next)
                gates_out(s, range(3, 8))
                split(q + 2, 3, width_next)
                halves(s, 8 * s + 8, GA)
                act.wait_ge(la_ready, s)
                act.activation(aa[:, :, :, :], la[:, :, :, :], ACT.Exp).then_inc(a_ready, 1)
                act.activation(tt[:, :, :, :], la[:, :, :, :], ACT.Tanh).then_inc(tanh_ready, 1)
                if conv is not None:
                    hi_of(uu[:, :, 0:S], uf[:, conv, :, :], u_made, s + 1, u_hi)
                act.wait_ge(one_minus, s)
                act.activation(tt[:, :, :, :], tt[:, :, :, :], ACT.Sqrt, scale=-1.0).then_inc(root_ready, 1)
                hi_of(hh[:, ds(4 * s - 4, 4), 0:S], la[:, 0, :, :], h_sum, s + 1, h_hi)

            with act.Fori(0, 2) as i:
                for k in range(2):
                    lru_strip(2 * i + 1 + k, N10, (k + 1) % 2)
            lru_strip(5, N8, None)

            def plain(q, e, group, nout=SN):
                splits(q + 1)
                splits(q + 2)
                halves(e, 4 * q + 8, group, nout)

            plain(12, 6, GB)
            with act.Fori(0, 3) as i:
                plain(4 * i + 14, 2 * i + 7, GA)
                plain(4 * i + 16, 2 * i + 8, GB)
            with act.Fori(0, 2) as i:
                for k in range(2):
                    plain(4 * i + 26 + 2 * k, 2 * i + 13 + k, psum[k])
                    hi_of(vv[:, ds(8 * i + 4 * k, 4), 0:S], v32[:, ds(8 * i + 4 * k, 4), :],
                          vg_made, 2 * i + k + 1, vg_hi)
            with act.Fori(0, 4) as i:
                q, e = 8 * i + 34, 4 * i + 17
                for k in range(4):
                    splits(q + 2 * k + 1, N10 if k == 1 else N8)
                    splits(q + 2 * k + 2, N10 if k == 0 else N8)
                    halves(e + k, 4 * (q + 2 * k) + 8, psum[k % 2])
                    if k % 2 == 0:
                        act.wait_ge(strip_out, e + k + 1)
                        act.activation(hid[:, 0, :, :], hid[:, 0, :, :], ACT.Sigmoid).then_inc(gl_sig, 1)
            for b in range(4):
                hi_of(mx[:, 4 * b:4 * b + 4, 0:S], m32[:, 4 * b:4 * b + 4, :], m_made, 4, m_hi)
            with act.Fori(0, 2) as i:
                plain(4 * i + 66, 2 * i + 33, GA)
                plain(4 * i + 68, 2 * i + 34, GB)

            def norm(n, src, centred, base, ready):
                if centred:
                    act.wait_ge(nsum[n], 1)
                    act.activation(mean[:, :], GA[:, 0, 0:S], ACT.Copy, scale=1.0 / D).then_inc(nmean[n], 1)
                for b in range(4):
                    ready(b)
                    act.activation(squares[:, 4 * b:4 * b + 4, :], src[:, 4 * b:4 * b + 4, :],
                                   ACT.Square).then_inc(nsq[n], 1)
                act.wait_ge(nvar[n], 1)
                act.activation(sdev[:, :], GA[:, 1, 0:S], ACT.Sqrt, scale=1.0 / D,
                               bias=eps[:, 0:1] if centred else eps[:, 1:2]).then_inc(nsd[n], 1)
                if base is not None:
                    for b in range(4):
                        hi_of(xx[:, 4 * b:4 * b + 4, 0:S], hnorm[:, b % 2, :, :], nh[n], b + 1, xx_hi)

            norm(0, zz, True, 4, lambda b: act.wait_ge(ncent[0], b + 1))
            with act.Fori(0, 8) as i:
                q, e = 8 * i + 74, 6 * i + 37
                for k in range(2):
                    plain(q + 2 * k, e + k, psum[k])
                    hi_of(ff[:, 4 * k:4 * k + 4, 0:S], hid[:, k, :, :], ff_made, 2 * i + k + 1, ff_hi)
                for j in range(4):
                    splits(q + 5 + j)
                    halves(e + 2 + j, 4 * (q + 4 + j) + 4, psum[j % 2])
            norm(1, res, True, None, lambda b: act.wait_ge(ncent[1], b + 1))
            norm(2, res, False, 8, lambda b: act.wait_ge(nh[1], b + 1))
            plain(138, 85, GA)
            plain(140, 86, GB)
            act.wait_ge(strip_out, 87)
            act.activation(qkv[:, 4:8, :], qkv[:, 4:8, :], ACT.Sigmoid).then_inc(bg_sig, 1)
            with act.Fori(0, 2) as i:
                for k in range(2):
                    plain(4 * i + 2 * k + 142, 2 * i + k + 87, psum[k])
            act.activation(squares[:, 0:8, :], qkv[:, 8:16, :], ACT.Square).then_inc(qk_sq, 1)
            plain(150, 91, GA)
            splits(153)
            halves(92, 4 * 153, GB, 2)
            act.wait_ge(strip_out, 93)
            act.activation(squares[:, 8:16, :], qkv[:, 20:28, :], ACT.Square).then_inc(qk_sq, 1)
            act.wait_ge(b_made, 4)
            act.activation(sq_last[:, :], qkv[:, 28, :], ACT.Square).then_inc(qk_sq, 1)
            act.wait_ge(b_sum, 1)
            act.activation(bmean[:, :], GA[:, 3, 0:S], ACT.Copy, scale=1.0 / (4 * P)).then_inc(b_mean, 1)
            act.wait_ge(qk_ssq, 1)
            act.activation(ssd[:, :, :, :].rearrange("p b n h -> p (b n h)"), GB[:, 3, 0:68], ACT.Sqrt,
                           scale=1.0 / HD, bias=eps[:, 1:2]).then_inc(qk_sd, 1)
            act.wait_ge(b_cent, 1)
            act.activation(bsq[:, :, :], bconv[:, :, :], ACT.Square).then_inc(b_sq, 1)
            act.wait_ge(vt_psum, 1)
            vt_rows = vt[:, :, :, :].rearrange("p b n c -> p (b n c)")
            act.activation(vt_rows[:, 0:1024].rearrange("p (b c) -> p b c", b=2), GA[:, 0:2, :], ACT.Copy)
            act.activation(vt_rows[:, 1024:1280], GA[:, 2, 0:S], ACT.Copy).then_inc(vt_out, 1)
            act.wait_ge(b_var, 1)
            act.activation(bsdev[:, :], GA[:, 3, S:2 * S], ACT.Sqrt, scale=1.0 / (4 * P), bias=eps[:, 1:2]
                           ).then_inc(b_sd, 1)
            act.wait_ge(b_norm, 1)
            act.activation(bconv[:, :, :], bconv[:, :, :], ACT.Silu).then_inc(b_silu, 1)
            hi_of(xx[:, 4:8, 0:S], bconv[:, :, :], b_silu, 1, xx_hi)

            def exps(n):
                act.wait_ge(peak_ready, n + 1)
                b = n % 2
                for hd in range(2):
                    for blk, cols in ((0, slice(0, P)), (1, slice(P, 3 * P))):
                        last = act.activation(probs[:, b, hd, cols], probs[:, b, hd, cols], ACT.Exp,
                                              bias=negm[:, b, hd, blk:blk + 1], accum_out=rsum[:, b, hd, blk:blk + 1])
                if PAIRS[n][3]:
                    for hd in range(2):
                        c = COL["sinks"] + n - 4 + 8 * hd
                        last = act.activation(sink[:, b, hd, :], negm[:, b, hd, :], ACT.Exp, bias=prm[:, c:c + 1])
                last.then_inc(exp_done, 1)

            exps(0)
            for n in range(13):
                if n < 11:
                    exps(n + 1)
                if n >= 1:
                    act.wait_ge(o_psum, n)
                    act.activation(xx[:, mix_tile(n - 1), 0:S], GB[:, 2 + (n - 1) % 2, 0:S], ACT.Copy).then_inc(xx_hi, 1)
                if n < 12:
                    act.wait_ge(pt_psum, n + 1)
                    if n >= 2:
                        act.wait_ge(o_psum, n - 1)
                    act.activation(probs_t[:, n % 2, :, :], GB[:, 0:2, 0:3 * P], ACT.Copy).then_inc(pt_out, 1)
            with act.Fori(0, 2) as i:
                for k in range(2):
                    plain(4 * i + 2 * k + 153, 2 * i + k + 93, psum[k])
            norm(3, res, False, 25, lambda b: act.wait_ge(strip_out, 94 + b))

            def gate_strip(q, e, n):
                plain(q, e, GA)
                act.wait_ge(strip_out, e + 1)
                act.activation(hid[:, 0, :, :], hid[:, 0, :, :], ACT.Silu).then_inc(gate_act, 1)

            def up_strip(q, e, n, more=True):
                splits(q + 1)
                if more:
                    splits(q + 2)
                halves(e, 4 * q + 8, GB)
                hi_of(ff[:, 0:4, 0:S], hid[:, 1, :, :], ff_made, 17 + n, ff_hi)

            gate_strip(161, 97, 0)
            up_strip(163, 98, 0)
            with act.Fori(0, 10) as i:
                q, e = 6 * i + 165, 6 * i + 99
                gate_strip(q, e, i + 1)
                for j in range(4):
                    splits(q + 3 + j // 2, N8, (0, 1) if j % 2 == 0 else (2, 3))
                    halves(e + 1 + j, 4 * q + 8 + 2 * j + 2, psum[(j + 1) % 2])
                up_strip(q + 4, e + 5, i + 1)
            for j in range(4):
                if j < 2:
                    splits(226, N8, (0, 1) if j == 0 else (2, 3))
                halves(159 + j, 4 * 225 + 2 * j + 2, psum[j % 2])

        @block.vector
        def _(dve):
            own = Steps(dve, dve_step)

            def lo(q, r, width=N8):
                dve.wait_ge(hi_done, 4 * q + r + 1)
                if not (isinstance(q, int) and q == 0):
                    dve.wait_ge(pe_piece, 4 * q + r - 3)
                dve.tensor_tensor(w_lo[:, r, 0:width], w_raw[:, r, 0:width], w_hi[:, r, 0:width].bitcast(F32),
                                  ALU.subtract).then_inc(lo_vec, 1)

            def los(q, width=N8, slots=(0, 2)):
                for r in slots:
                    lo(q, r, width)

            def total(e, group, dst, nout=SN):
                dve.wait_ge(half_out, e + 1)
                dve.tensor_tensor(dst, group[:, 0:nout, 0:S], half[:, 0:nout, :], ALU.add).then_inc(strip_out, 1)
                dve.wait_ge(strip_out, e + 1)

            def add_total(e, group, dst):
                dve.wait_ge(half_out, e + 1)
                own.done(dve.tensor_tensor(dst, group[:, :, 0:S], dst, ALU.add))
                own.need()
                dve.tensor_tensor(dst, half[:, :, :], dst, ALU.add).then_inc(strip_out, 1)

            def lo_of(dst, src, hi, n, hi_sem, done):
                dve.wait_ge(hi_sem, n)
                dve.tensor_tensor(dst, src, hi.bitcast(F32), ALU.subtract).then_inc(done, 1)

            def column(name, n):
                return prm[:, ds(COL[name] + n, 1)]

            dve.memset(eps[:, 0:1], LN_EPS)
            dve.memset(eps[:, 1:2], RMS_EPS)
            dve.memset(padded[:, :, :], 0.0).then_inc(gate_out, SN)
            dve.memset(ones[:, :], 1.0).then_inc(const_ready, 1)
            los(0)
            for b in range(4):
                lo_of(xx[:, 4 * b:4 * b + 4, S:2 * S], zz[:, 4 * b:4 * b + 4, :], xx[:, 4 * b:4 * b + 4, 0:S],
                      b + 1, xx_hi, xx_lo)
            lam = prm[:, COL["lam"]:COL["lam"] + 2 * HT]
            neg, sq, poly = series[:, 0, :], series[:, 1, :], series[:, 2, :]
            dve.wait_ge(params_in, 16)
            own.done(dve.tensor_scalar(neg, lam, -1.0, None, ALU.mult))
            own.need()
            dve.tensor_tensor(decay[:, :], lam, neg, ALU.max).then_inc(const_ready, 1)
            own.done(dve.tensor_scalar(neg, neg, 0.0, None, ALU.max))
            dve.wait_ge(exp_lam, 1)
            own.done(dve.tensor_scalar(sq, decay[:, :], 2.0, None, ALU.add))
            own.need()
            own.done(dve.reciprocal(poly, sq))
            own.need()
            own.done(dve.tensor_tensor(decay[:, :], decay[:, :], poly, ALU.mult))
            own.need()
            own.done(dve.tensor_tensor(sq, decay[:, :], decay[:, :], ALU.mult))
            own.need()
            own.done(dve.tensor_scalar(poly, sq, 1.0 / 17, 1.0 / 15, ALU.mult, ALU.add))
            for odd in (13, 11, 9, 7, 5, 3, 1):
                own.need()
                own.done(dve.tensor_tensor(poly, poly, sq, ALU.mult))
                own.need()
                own.done(dve.tensor_scalar(poly, poly, 1.0 / odd, None, ALU.add))
            own.need()
            own.done(dve.tensor_tensor(poly, poly, decay[:, :], ALU.mult))
            own.need()
            own.done(dve.scalar_tensor_tensor(poly, poly, 2.0, neg, ALU.mult, ALU.add))
            own.need()
            own.done(dve.tensor_scalar(decay[:, :], poly, -LRU_C, None, ALU.mult))
            own.done(dve.tensor_tensor(gqk[:, 0:1], column("aq_g", 0), column("ak_g", 0), ALU.mult))
            own.done(dve.tensor_tensor(gqk[:, 1:2], column("cq_g", 0), column("ck_g", 0), ALU.mult))
            dve.memset(sink[:, :, :, :], 0.0).then_inc(h_sum, 1)
            los(1)
            los(2, N10)

            def conv_u(s, e, buf):
                total(e, GA, padded[:, :, 2:2 + S])
                taps = []
                for hd in range(SN):
                    taps.append(own.done(dve.tensor_scalar(
                        uf[:, buf, hd, :], padded[:, hd, 0:S], column("lru_w", hd + 4 * s), column("lru_b", hd + 4 * s),
                        ALU.mult, ALU.add)))
                for k in range(1, 4):
                    for hd in range(SN):
                        own.need(taps[hd])
                        ins = dve.scalar_tensor_tensor(
                            uf[:, buf, hd, :], padded[:, hd, k:k + S], column("lru_w", k * HT + hd + 4 * s),
                            uf[:, buf, hd, :], ALU.mult, ALU.add)
                        if k == 3 and hd == SN - 1:
                            ins.then_inc(u_made, 1)
                        else:
                            taps[hd] = own.done(ins)

            conv_u(0, 0, 0)
            lo_of(uu[:, :, S:2 * S], uf[:, 0, :, :], uu[:, :, 0:S], 1, u_hi, u_lo)

            def lru_strip(s, width_next, conv):
                q = 2 * s
                los(q + 1, N10)
                los(q + 2, width_next)
                dve.wait_ge(gate_out, 8 * s + 4)
                for hd in range(SN):
                    for way in range(2):
                        c = way * HT + hd - 4 + 4 * s
                        last = dve.tensor_scalar(la[:, way, hd, :], gates[:, hd, way, 0, :], decay[:, ds(c, 1)],
                                                 None, ALU.mult)
                last.then_inc(la_ready, 1)
                if conv is not None:
                    conv_u(s, s, conv)
                else:
                    total(s, GA, hid[:, 1, :, :])
                dve.wait_ge(sq_ready, s)
                dve.wait_ge(tanh_ready, s)
                for way in range(2):
                    last = dve.scalar_tensor_tensor(tt[:, way, :, :], gates[:, :, way, 0, :], 1.0, tt[:, way, :, :],
                                                    ALU.add, ALU.mult)
                last.then_inc(one_minus, 1)
                if conv is not None:
                    lo_of(uu[:, :, S:2 * S], uf[:, conv, :, :], uu[:, :, 0:S], s + 1, u_hi, u_lo)
                dve.wait_ge(root_ready, s)
                dve.wait_ge(iu_ready, s)
                gx = [own.done(dve.tensor_tensor(tt[:, way, :, :], tt[:, way, :, :], gates[:, :, way, 1, :], ALU.mult))
                      for way in range(2)]
                for way, order in ((0, slice(None)), (1, slice(None, None, -1))):
                    own.need(gx[way])
                    for hd in range(SN):
                        own.done(dve.tensor_tensor_scan(la[:, way, hd, order], aa[:, way, hd, order],
                                                        tt[:, way, hd, order], 0.0, ALU.mult, ALU.add))
                own.need()
                dve.tensor_tensor(la[:, 0, :, :], la[:, 0, :, :], la[:, 1, :, :], ALU.add).then_inc(h_sum, 1)
                blocks = ds(4 * s - 4, 4)
                lo_of(hh[:, blocks, S:2 * S], la[:, 0, :, :], hh[:, blocks, 0:S], s, h_hi, h_lo)

            LRU_STEPS = 15 + 10
            with dve.Fori(0, 2) as i:
                own.enter(i, 2 * LRU_STEPS)
                for k in range(2):
                    lru_strip(2 * i + 1 + k, N10, (k + 1) % 2)
                own.leave(2)
            lru_strip(5, N8, None)

            def plain(q, e, group, dst, nout=SN):
                los(q + 1)
                los(q + 2)
                total(e, group, dst, nout)

            def conv_v(b):
                taps = []
                for j in range(SN):
                    taps.append(own.done(dve.tensor_scalar(
                        v32[:, ds(4 * b + j, 1), :], padded[:, j:j + 1, 1:1 + S], column("sc_w", j + 4 * b),
                        column("sc_b", j + 4 * b), ALU.mult, ALU.add)))
                for k in range(1, 3):
                    for j in range(SN):
                        own.need(taps[j])
                        taps[j] = own.done(dve.scalar_tensor_tensor(
                            v32[:, ds(4 * b + j, 1), :], padded[:, j:j + 1, k + 1:k + 1 + S],
                            column("sc_w", k * KT + j + 4 * b), v32[:, ds(4 * b + j, 1), :], ALU.mult, ALU.add))

            def c_times_x():
                own.done(dve.tensor_tensor(padded[:, :, 2:2 + S], hid[:, 0, :, :], hid[:, 1, :, :], ALU.mult))
                own.need()

            plain(12, 6, GB, hid[:, 0, :, :])
            c_times_x()
            conv_v(0)
            with dve.Fori(0, 3) as i:
                own.enter(i, 13)
                plain(4 * i + 14, 2 * i + 7, GA, hid[:, 1, :, :])
                plain(4 * i + 16, 2 * i + 8, GB, hid[:, 0, :, :])
                c_times_x()
                conv_v(i + 1)
                own.leave(3)
            own.need()
            with dve.Fori(0, 2) as i:
                for k in range(2):
                    plain(4 * i + 26 + 2 * k, 2 * i + 13 + k, psum[k], hid[:, 0, :, :])
                    blocks = ds(8 * i + 4 * k, 4)
                    dve.tensor_tensor(v32[:, blocks, :], v32[:, blocks, :], hid[:, 0, :, :], ALU.mult).then_inc(vg_made, 1)
                    lo_of(vv[:, blocks, S:2 * S], v32[:, blocks, :], vv[:, blocks, 0:S], 2 * i + k + 1, vg_hi, vg_lo)
            with dve.Fori(0, 4) as i:
                own.enter(i, 2)
                q, e = 8 * i + 34, 4 * i + 17
                block_ = m32[:, ds(4 * i, 4), :]
                for k in range(4):
                    los(q + 2 * k + 1, N10 if k == 1 else N8)
                    los(q + 2 * k + 2, N10 if k == 0 else N8)
                    total(e + k, psum[k % 2], hid[:, k % 2, :, :])
                    if k == 1:
                        dve.wait_ge(gl_sig, 2 * i + 1)
                        own.done(dve.tensor_tensor(block_, hid[:, 0, :, :], hid[:, 1, :, :], ALU.mult))
                    if k == 3:
                        dve.wait_ge(gl_sig, 2 * i + 2)
                        own.done(dve.tensor_tensor(hid[:, 1, :, :], hid[:, 0, :, :], hid[:, 1, :, :], ALU.mult))
                        own.need()
                        dve.tensor_tensor(block_, block_, hid[:, 1, :, :], ALU.add).then_inc(m_made, 1)
                own.leave(4)
            for b in range(4):
                blocks = slice(4 * b, 4 * b + 4)
                lo_of(mx[:, blocks, S:2 * S], m32[:, blocks, :], mx[:, blocks, 0:S], b + 1, m_hi, m_lo)
            with dve.Fori(0, 2) as i:
                own.enter(i, 2)
                for k in range(2):
                    blocks = ds(8 * i + 4 * k, 4)
                    plain(4 * i + 2 * k + 66, 2 * i + k + 33, psum[k], zz[:, blocks, :])
                    own.done(dve.scalar_tensor_tensor(zz[:, blocks, :], xx[:, blocks, 0:S].bitcast(F32), ALPHA,
                                                      zz[:, blocks, :], ALU.mult, ALU.add))
                    own.need()
                    dve.scalar_tensor_tensor(zz[:, blocks, :], xx[:, blocks, S:2 * S].bitcast(F32), ALPHA,
                                             zz[:, blocks, :], ALU.mult, ALU.add).then_inc(z_made, 1)
                own.leave(2)

            def each_token(t):
                return t[:, :].unsqueeze(1).to_broadcast([P, SN, S])

            def centre(n, src):
                dve.wait_ge(nmean[n], 1)
                for b in range(4):
                    dve.tensor_tensor(src[:, 4 * b:4 * b + 4, :], src[:, 4 * b:4 * b + 4, :], each_token(mean),
                                      ALU.subtract).then_inc(ncent[n], 1)

            def inverse(n):
                dve.wait_ge(nsd[n], 1)
                own.done(dve.reciprocal(rstd[:, :], sdev[:, :]))

            def normed(n, src, base, gain, shift):
                inverse(n)
                own.need()
                for b in range(5):
                    if b < 4:
                        h = hnorm[:, b % 2, :, :]
                        if b >= 2:
                            dve.wait_ge(xx_lo, base + b - 1)
                        if n == 0 and b >= 2:
                            dve.wait_ge(res_seed, b - 1)
                        own.done(dve.tensor_tensor(h, src[:, 4 * b:4 * b + 4, :], each_token(rstd), ALU.mult))
                        own.need()
                        for j in range(SN):
                            t = 4 * b + j
                            last = dve.tensor_scalar(h[:, j, :], h[:, j, :], column(gain, t),
                                                     column(shift, t) if shift else None, ALU.mult,
                                                     *([ALU.add] if shift else []))
                        last.then_inc(nh[n], 1)
                    if b >= 1:
                        c = b - 1
                        blocks = slice(4 * c, 4 * c + 4)
                        lo_of(xx[:, blocks, S:2 * S], hnorm[:, c % 2, :, :], xx[:, blocks, 0:S],
                              base + c + 1, xx_hi, xx_lo)

            centre(0, zz)
            normed(0, zz, 4, "ln1_g", "ln1_b")
            with dve.Fori(0, 8) as i:
                own.enter(i, 2 * 4 + 4)
                q, e = 8 * i + 74, 6 * i + 37
                for k in range(2):
                    plain(q + 2 * k, e + k, psum[k], hid[:, k, :, :])
                    for j in range(SN):
                        own.done(dve.tensor_scalar(hid[:, k, j, :], hid[:, k, j, :], column("b1", 4 * k + j + 8 * i),
                                                   0.0, ALU.add, ALU.max))
                    own.need()
                    dve.tensor_tensor(hid[:, k, :, :], hid[:, k, :, :], hid[:, k, :, :], ALU.mult).then_inc(ff_made, 1)
                    lo_of(ff[:, 4 * k:4 * k + 4, S:2 * S], hid[:, k, :, :], ff[:, 4 * k:4 * k + 4, 0:S],
                          2 * i + k + 1, ff_hi, ff_lo)
                dve.wait_ge(res_seed, 4)
                for j in range(4):
                    los(q + 5 + j)
                    add_total(e + 2 + j, psum[j % 2], res[:, 4 * j:4 * j + 4, :])
                own.leave(8)
            centre(1, res)
            inverse(1)
            own.need()
            for b in range(4):
                h = res[:, 4 * b:4 * b + 4, :]
                own.done(dve.tensor_tensor(h, h, each_token(rstd), ALU.mult))
                own.need()
                for j in range(SN):
                    last = dve.tensor_scalar(h[:, j, :], h[:, j, :], column("ln2_g", 4 * b + j),
                                             column("ln2_b", 4 * b + j), ALU.mult, ALU.add)
                last.then_inc(nh[1], 1)
            normed(2, res, 8, "n1_g", None)
            plain(138, 85, GA, qkv[:, 0:4, :])
            plain(140, 86, GB, qkv[:, 4:8, :])
            dve.memset(bpad[:, :, :], 0.0).then_inc(bg_sum, 1)
            dve.wait_ge(bg_sum, 1)
            dve.wait_ge(bg_sig, 1)
            own.done(dve.tensor_tensor(bpad[:, :, 30:30 + S], qkv[:, 0:4, :], qkv[:, 4:8, :], ALU.mult))

            def taps2(tile, ks):
                for k in ks:
                    own.need()
                    y = bconv[:, ds(tile, 1), :]
                    x = bpad[:, ds(tile, 1), k:k + S]
                    if k == 0:
                        ins = dve.tensor_scalar(y, x, column("cv_w", tile), column("cv_b", tile), ALU.mult, ALU.add)
                    else:
                        ins = dve.scalar_tensor_tensor(y, x, column("cv_w", tile + 4 * k), y, ALU.mult, ALU.add)
                    if k == TAPS2 - 1:
                        ins.then_inc(b_made, 1)
                    else:
                        own.done(ins)

            with dve.Fori(0, 2) as i:
                own.enter(i, 60)
                for k in range(2):
                    q, e, tile = 4 * i + 2 * k + 142, 2 * i + k + 87, 2 * i + k
                    lo(q + 1, 0)
                    taps2(tile, range(0, 8))
                    lo(q + 1, 2)
                    taps2(tile, range(8, 16))
                    lo(q + 2, 0)
                    taps2(tile, range(16, 24))
                    lo(q + 2, 2)
                    total(e, psum[k], qkv[:, ds(8 + 8 * i + 4 * k, 4), :])
                    taps2(tile, range(24, 31))
                own.leave(2)
            plain(150, 91, GA, qkv[:, 24:28, :])
            los(153)
            total(92, GB, qkv[:, 28:30, :], 2)
            dve.wait_ge(b_mean, 1)
            dve.tensor_tensor(bconv[:, :, :], bconv[:, :, :], each_token(bmean), ALU.subtract).then_inc(b_cent, 1)
            dve.wait_ge(qk_sd, 1)
            flat = "p b n h -> p (b n h)"
            own.done(dve.reciprocal(rn[:, :, :, :].rearrange(flat), ssd[:, :, :, :].rearrange(flat)))
            own.need()
            own.done(dve.tensor_scalar(rq[:, :, :, :].rearrange(flat), rn[:, :, :, :].rearrange(flat), HD ** -0.5, None,
                                       ALU.mult))
            for blk in range(2):
                for at, n, count in ((0, 4, 4), (4, 16, 1)):
                    last = dve.tensor_copy(rn_rows[:, blk, at:at + count, :].rearrange("p n (h d) -> p n h d", h=2),
                                           rn[:, blk, n:n + count, :].unsqueeze(3).to_broadcast([P, count, 2, HD]))
            last.then_inc(rows_ready, 1)
            dve.wait_ge(k_rows, 1)
            for n in range(5):
                tile = 12 + n if n < 4 else 28
                last = dve.scalar_tensor_tensor(qkv[:, tile, :], qkv[:, tile, :], gqk[:, n // 4:n // 4 + 1],
                                                GB[:, n // 2, (n % 2) * S:(n % 2) * S + S], ALU.mult, ALU.mult)
            last.then_inc(k_ready, 1)
            dve.wait_ge(b_sd, 1)
            own.done(dve.reciprocal(bmean[:, :], bsdev[:, :]))
            own.need()
            own.done(dve.tensor_tensor(bconv[:, :, :], bconv[:, :, :], each_token(bmean), ALU.mult))
            own.need()
            for j in range(4):
                last = dve.tensor_scalar(bconv[:, j, :], bconv[:, j, :], column("cln_g", j), column("cln_b", j),
                                         ALU.mult, ALU.add)
            last.then_inc(b_norm, 1)
            lo_of(xx[:, 4:8, S:2 * S], bconv[:, :, :], xx[:, 4:8, 0:S], 13, xx_hi, xx_lo)
            dve.wait_ge(const_in_sem, 16)

            def prepare(n):
                qt, _, _, kind = PAIRS[n]
                idx, b = NORMED.index(qt), n % 2
                dve.wait_ge(score_psum, n + 1)
                if n >= 2:
                    dve.wait_ge(pt_psum, n - 1)
                for hd in range(2):
                    for blk, cols in ((0, slice(0, P)), (1, slice(P, 3 * P))):
                        last = dve.scalar_tensor_tensor(probs[:, b, hd, cols], GA[:, 2 * b + hd, cols],
                                                        rq[:, blk, idx, hd:hd + 1], masks[:, kind, cols],
                                                        ALU.mult, ALU.add)
                last.then_inc(score_out, 1)
                dve.wait_ge(score_out, n + 1)
                own.done(dve.reduce_max(peak[:, b, :, 0], probs[:, b, :, 0:P], AX.X))
                own.done(dve.reduce_max(peak[:, b, :, 1], probs[:, b, :, P:3 * P], AX.X))
                own.need()
                if kind == 0:
                    last = dve.tensor_scalar(negm[:, b, :, :], peak[:, b, :, :], -1.0, None, ALU.mult)
                else:
                    for hd in range(2):
                        last = dve.tensor_scalar(negm[:, b, hd, :], peak[:, b, hd, :], column("sinks", n - 4 + 8 * hd),
                                                 -1.0, ALU.max, ALU.mult)
                last.then_inc(peak_ready, 1)

            prepare(0)
            for n in range(13):
                if n < 11:
                    prepare(n + 1)
                if n < 12:
                    b = n % 2
                    dve.wait_ge(exp_done, n + 1)
                    if PAIRS[n][3]:
                        own.done(dve.tensor_tensor(rsum[:, b, :, :], rsum[:, b, :, :], sink[:, b, :, :], ALU.add))
                        own.need()
                    dve.reciprocal(rsum[:, b, :, :], rsum[:, b, :, :]).then_inc(rsum_ready, 1)
                if n >= 1:
                    lo_of(xx[:, mix_tile(n - 1), S:2 * S], GB[:, 2 + (n - 1) % 2, 0:S], xx[:, mix_tile(n - 1), 0:S],
                          13 + n, xx_hi, xx_lo)
            with dve.Fori(0, 2) as i:
                own.enter(i, 2)
                for k in range(2):
                    q = 4 * i + 2 * k + 153
                    los(q + 1)
                    los(q + 2)
                    add_total(2 * i + k + 93, psum[k], res[:, ds(8 * i + 4 * k, 4), :])
                own.leave(2)
            normed(3, res, 25, "n2_g", None)

            def gate_strip(q, e):
                plain(q, e, GA, hid[:, 0, :, :])

            def up_strip(q, e, n):
                plain(q, e, GB, hid[:, 1, :, :])
                dve.wait_ge(gate_act, n + 1)
                dve.tensor_tensor(hid[:, 1, :, :], hid[:, 1, :, :], hid[:, 0, :, :], ALU.mult).then_inc(ff_made, 1)
                lo_of(ff[:, 0:4, S:2 * S], hid[:, 1, :, :], ff[:, 0:4, 0:S], 17 + n, ff_hi, ff_lo)

            gate_strip(161, 97)
            up_strip(163, 98, 0)
            with dve.Fori(0, 10) as i:
                own.enter(i, 4)
                q, e = 6 * i + 165, 6 * i + 99
                gate_strip(q, e)
                for j in range(4):
                    lo(q + 3 + j // 2, 2 * (j % 2))
                    add_total(e + 1 + j, psum[(j + 1) % 2], res[:, 4 * j:4 * j + 4, :])
                up_strip(q + 4, e + 5, i + 1)
                own.leave(10)
            for j in range(4):
                if j < 2:
                    lo(226, 2 * j)
                add_total(159 + j, psum[j % 2], res[:, 4 * j:4 * j + 4, :])

        @block.gpsimd
        def _(pool):
            def lo(q, r, width=N8):
                pool.wait_ge(hi_done, 4 * q + r + 1)
                if not (isinstance(q, int) and q == 0):
                    pool.wait_ge(pe_piece, 4 * q + r - 3)
                pool.tensor_tensor(w_lo[:, r, 0:width], w_raw[:, r, 0:width], w_hi[:, r, 0:width].bitcast(F32),
                                   ALU.subtract).then_inc(lo_pool, 1)

            def los(q, width=N8, slots=(1, 3)):
                for r in slots:
                    lo(q, r, width)

            los(0)
            los(1)
            los(2, N10)

            def lru_strip(s, width_next, buf):
                q = 2 * s
                los(q + 1, N10)
                los(q + 2, width_next)
                pool.wait_ge(gate_out, 8 * s + 4)
                for way in range(2):
                    last = pool.tensor_tensor(gates[:, :, way, 1, :], gates[:, :, way, 1, :], uf[:, buf, :, :], ALU.mult)
                last.then_inc(iu_ready, 1)
                pool.wait_ge(a_ready, s)
                for way in range(2):
                    last = pool.tensor_tensor(gates[:, :, way, 0, :], aa[:, way, :, :], aa[:, way, :, :], ALU.mult)
                last.then_inc(sq_ready, 1)

            with pool.Fori(0, 2) as i:
                for k in range(2):
                    lru_strip(2 * i + 1 + k, N10, k)
            lru_strip(5, N8, 0)
            with pool.Fori(0, 22) as i:
                los(i + 13)
            with pool.Fori(0, 4) as i:
                for k, width in enumerate((N8, N10, N10, N8, N8, N8, N8, N8)):
                    los(8 * i + 35 + k, width)
            with pool.Fori(0, 8) as i:
                los(i + 67)
            for b in range(4):
                pool.wait_ge(nh[0], b + 1)
                for j in range(SN):
                    t = 4 * b + j
                    last = pool.tensor_scalar(res[:, t, :], hnorm[:, b % 2, j, :], ALPHA,
                                              prm[:, COL["b2"] + t:COL["b2"] + t + 1], ALU.mult, ALU.add)
                last.then_inc(res_seed, 1)
            with pool.Fori(0, 64) as i:
                los(i + 75)
            with pool.Fori(0, 15) as i:
                los(i + 139)
            for n in range(12):
                b = n % 2
                pool.wait_ge(rsum_ready, n + 1)
                for hd in range(2):
                    for blk, cols in ((0, slice(0, P)), (1, slice(P, 3 * P))):
                        last = pool.tensor_scalar(probs[:, b, hd, cols], probs[:, b, hd, cols],
                                                  rsum[:, b, hd, blk:blk + 1], None, ALU.mult)
                last.then_inc(p_ready, 1)
            with pool.Fori(0, 8) as i:
                los(i + 154)
            with pool.Fori(0, 65) as i:
                los(i + 162)


def mix_tile(n):
    return n if n < 4 else n + 4


def strips(w, width=SN * P, per=2):
    rows, cols = w.shape
    a = w.reshape(rows // (per * P), per, P, cols // width, width)
    return a.transpose(3, 0, 2, 1, 4).reshape(-1, P, per * width)


def tiles_of(w):
    rows, cols = w.shape
    return w.reshape(rows // P, P, cols // P, P).transpose(0, 2, 1, 3).reshape(-1, P, P)


def pieces10(tiles):
    return tiles.reshape(-1, 10, P, P).transpose(0, 2, 1, 3).reshape(-1, P, N10)


def columns(v):
    v = np.asarray(v).reshape(-1, P)
    return v.T


def lay_out(a):
    edges = np.cumsum([0, LRU_W, CONV_W, CONV_W, CONV_W, D, D])
    w = a["w_in"]
    w_lru, w_x, w_b, w_c, w_gl, w_gc = (w[:, edges[k]:edges[k + 1]] for k in range(6))
    strip = lambda m, s: m[:, SN * P * s:SN * P * (s + 1)]
    s8 = [strips(strip(w_lru, 0))]
    s10 = []
    for s in range(1, 6):
        main = strip(w_lru, s) if s < 5 else strip(w_x, 0)
        heads = slice(4 * (s - 1), 4 * s)
        ga = np.stack([a["lru_w_a"][:, heads], a["lru_w_x"][:, heads]], 2)
        s10.append(pieces10(np.concatenate([tiles_of(main), ga.transpose(1, 0, 2, 3, 4).reshape(-1, P, P)])))
    s8.append(strips(strip(w_c, 0)))
    for s in range(1, 4):
        s8 += [strips(strip(w_x, s)), strips(strip(w_c, s))]
    s8 += [strips(w_b)]
    for s in range(4):
        s8 += [strips(strip(w_gl, s)), strips(strip(w_gc, s)), strips(strip(a["w_conv_out"], s))]
        s10.append(pieces10(tiles_of(strip(a["w_lru_out"], s))))
    s8.append(strips(a["w_o"]))
    for i in range(8):
        rows = slice(8 * P * i, 8 * P * (i + 1))
        s8 += [strips(a["mlp_w1"][:, rows]), strips(a["mlp_w2"][rows])]
    w2 = a["w_in_2"][0]
    at = np.cumsum([0, 512, 512, 512, 512, 512, 1024, 128, 128])
    aq, ak, av, bu, bg, cq, ck, cv = (w2[:, at[k]:at[k + 1]] for k in range(8))
    cq = cq.reshape(D, 2, 8, HD).transpose(0, 2, 1, 3).reshape(D, C_HEADS * HD)
    s8.append(strips(np.concatenate([bu, bg, aq, ak, av, cq], 1)))
    s8.append(strips(np.concatenate([ck, cv], 1), 2 * P, 4))
    wo = a["w_out_2"][0]
    woc = wo[D // 2:].reshape(2, 8, HD, D).transpose(1, 0, 2, 3).reshape(D // 2, D)
    s8.append(strips(np.concatenate([wo[:D // 2], woc])))
    n2 = D_FF2 // (SN * P)
    gate, up = a["w_gate_2"][0], a["w_up_2"][0]
    down = lambda s: strips(a["w_down_2"][0][SN * P * s:SN * P * (s + 1)])
    s8 += [strips(strip(gate, 0)), strips(strip(up, 0))]
    for s in range(1, n2):
        s8 += [strips(strip(gate, s)), down(s - 1), strips(strip(up, s))]
    s8.append(down(n2 - 1))
    twice = lambda g: np.concatenate([g[0], g[0]])
    values = dict(
        lru_w=a["lru_conv_w"], lru_b=a["lru_conv_b"], b_a=a["lru_b_a"], b_x=a["lru_b_x"], lam=a["lru_lambda"],
        sc_w=a["sc_conv_w"], sc_b=a["sc_conv_b"], ln1_g=a["ln1_g"], ln1_b=a["ln1_b"], b1=a["mlp_b1"], b2=a["mlp_b2"],
        ln2_g=a["ln2_g"], ln2_b=a["ln2_b"], n1_g=a["norm1_g_2"], aq_g=twice(a["a_q_g_2"]), ak_g=twice(a["a_k_g_2"]),
        cq_g=twice(a["c_q_g_2"]), ck_g=twice(a["c_k_g_2"]), cv_w=a["conv_w_2"][0], cv_b=a["conv_b_2"],
        cln_g=a["conv_ln_g_2"], cln_b=a["conv_ln_b_2"], n2_g=a["norm2_g_2"],
        sinks=np.repeat(a["c_sinks_2"][0], P))
    prm = np.concatenate([columns(values[name]) for name, _ in PARAM_SIZES], 1)
    x = a["x"][0].T.reshape(KT, P, S).transpose(1, 0, 2)
    return dict(x=x, prm=prm, const=constants(), w8=np.concatenate(s8), w10=np.concatenate(s10))


def constants():
    q, k = np.arange(S)[:, None], np.arange(S)[None, :]
    dist = q - k
    reached = sum(((dist >= 0) & (dist <= w) & (dist % d == 0)).astype(int)
                  for w, d in ((128, 1), (512, 4), (2048, 16)))
    mask_a = np.where(reached > 0, np.log(np.maximum(reached, 1)), -1e30)
    mask_c = np.where((dist >= 0) & (dist < 128), 0.0, -1e30)
    blocks = [np.concatenate([m[:P, :P], m[P:, :P], m[P:, P:]], 1) for m in (mask_a, mask_c)]
    halves = (np.arange(P)[:, None] // HD == np.arange(2)[None, :]).astype(float)
    return np.concatenate([np.eye(P), *blocks, halves], 1).astype(np.float32)


def kernel(**inputs):
    import concourse.bacc as bacc
    from concourse.bass_utils import run_bass_kernel_spmd

    arrays = {k: np.ascontiguousarray(v) for k, v in lay_out({k: np.asarray(v) for k, v in inputs.items()}).items()}
    nc = bacc.Bacc("TRN2", target_bir_lowering=False, num_devices=1)
    aps = [nc.dram_tensor(f"{k}_dram", arrays[k].shape, F32, kind="ExternalInput").ap()
           for k in ("x", "prm", "const", "w8", "w10")]
    out = nc.dram_tensor("out_dram", (P, KT, S), F32, kind="ExternalOutput").ap()
    build(nc, *aps, out)
    got = run_bass_kernel_spmd(nc, [{f"{k}_dram": v for k, v in arrays.items()}], core_ids=[0])
    y = got.results[0]["out_dram"]
    return np.ascontiguousarray(y.transpose(2, 1, 0)).reshape(1, S, D)
```

```python
from contextlib import ExitStack

import numpy as np
import concourse.bass as bass
from concourse import mybir

P = 128
S = 256
D = 2048
LRU_W, LRU_HEADS = 2560, 20
CONV_W = 2048
D_FF = 4 * D
D_FF2 = 5632
A_HEADS, C_HEADS, C_KV, HD = 8, 16, 2, 64
TAPS2 = 31
ALPHA = float(2 ** 0.25)
LN_EPS, RMS_EPS = 1e-5, 1e-6
KT = D // P
HT = LRU_W // P
SN = 4
N8, N10 = 8 * P, 10 * P
RING = 4
LRU_C = 8.0

ALU = mybir.AluOpType
ACT = mybir.ActivationFunctionType
AX = mybir.AxisListType
F32 = mybir.dt.float32
F32R = mybir.dt.float32r

PARAM_SIZES = [
    ("lru_w", 4 * HT), ("lru_b", HT), ("b_a", 2 * HT), ("b_x", 2 * HT), ("lam", 2 * HT),
    ("sc_w", 3 * KT), ("sc_b", KT), ("ln1_g", KT), ("ln1_b", KT), ("b1", D_FF // P), ("b2", KT),
    ("ln2_g", KT), ("ln2_b", KT), ("n1_g", KT), ("aq_g", 1), ("ak_g", 1), ("cq_g", 1), ("ck_g", 1),
    ("cv_w", 4 * TAPS2), ("cv_b", 4), ("cln_g", 4), ("cln_b", 4), ("n2_g", KT), ("sinks", C_HEADS),
]
COL = {}
_at = 0
for _name, _n in PARAM_SIZES:
    COL[_name] = _at
    _at += _n
NPARAM = _at
NCONST = P + 2 * 3 * P + 2




class Steps:

    def __init__(self, eng, sem):
        self.eng, self.sem, self.base, self.n = eng, sem, 0, 0

    def done(self, ins):
        ins.then_inc(self.sem, 1)
        self.n += 1
        return self.n

    def need(self, n=None):
        self.eng.wait_ge(self.sem, self.base + (self.n if n is None else n))

    def enter(self, i, per):
        self.before, self.per = self.base + self.n, per
        self.base, self.n = self.before + i * per, 0

    def leave(self, times):
        assert self.n == self.per, (self.n, self.per)
        self.base, self.n = self.before + times * self.per, 0


def outs(n):
    return n + 1


def ds(a, n):
    return slice(a, a + n) if isinstance(a, int) else bass.ds(a, n)


def build(nc, x_in, prm_in, const_in, w8, w10, out):
    with ExitStack() as ctx:
        def sb(name, shape, dt=F32, where=ctx):
            return where.enter_context(nc.sbuf_tensor(name, shape, dt))

        def sem(name):
            return ctx.enter_context(nc.semaphore(name))

        w_raw = sb("w_raw", [P, RING, N10])
        w_hi = sb("w_hi", [P, RING, N10], F32R)
        w_lo = sb("w_lo", [P, RING, N10], F32R)
        xx = sb("xx", [P, KT, 2 * S], F32R)
        half = sb("half", [P, SN, S])
        prm = sb("prm", [P, NPARAM])
        const = sb("const", [P, NCONST])
        ident, masks = const[:, 0:P], const[:, P:P + 768].rearrange("p (m n) -> p m n", m=2)
        pair_ones = const[:, 896:898]
        ones = sb("ones", [P, P])
        eps = sb("eps", [P, 2])
        warm = sb("warm", [P, 2])
        decay = sb("decay", [P, 2 * HT])
        padded = sb("padded", [P, SN, S + 4])

        def region(*tensors):
            with ExitStack() as stack:
                return [sb(n, shape, dt, stack) for n, shape, dt in tensors]

        def in_turn(name, size, *phases):
            made = [region(*tensors) for tensors in phases]
            sb(name, [P, size])
            return made

        (series, _, b3), (hh,), (mx,), (res, bconv, probs, probs_t, vt) = in_turn(
            "region_h", HT * 2 * S,
            [("series", [P, 3, 2 * HT], F32), ("low_h", [P, 16 * 2 * S - 6 * HT], F32),
             ("b3", [P, SN, S], F32)],
            [("hh", [P, HT, 2 * S], F32R)],
            [("mx", [P, KT, 2 * S], F32R)],
            [("res", [P, KT, S], F32),
             ("bconv", [P, 4, S], F32),
             ("probs", [P, 3, 2, 3 * P], F32),
             ("probs_t", [P, 2, 2, 3 * P], F32),
             ("vt", [P, 2, 5, P], F32)])
        (v32,), (m32,), (squares,), (rn_rows,), (ff,) = in_turn(
            "region_g", KT * S,
            [("v32", [P, KT, S], F32)],
            [("m32", [P, KT, S], F32)],
            [("squares", [P, KT, S], F32)],
            [("rn_rows", [P, 2, 5, P], F32)],
            [("ff", [P, 8, 2 * S], F32R)])
        (gates, aa, tt), (vv,), (zz, mean, rstd, sdev, hnorm), (qkv,), (x2,) = in_turn(
            "region_v", KT * 2 * S,
            [("gates", [P, SN, 2, 2, S], F32),
             ("aa", [P, 2, SN, S], F32),
             ("tt", [P, 2, SN, S], F32)],
            [("vv", [P, KT, 2 * S], F32R)],
            [("zz", [P, KT, S], F32), ("mean", [P, S], F32), ("rstd", [P, S], F32),
             ("sdev", [P, S], F32), ("hnorm", [P, 2, SN, S], F32)],
            [("qkv", [P, 30, S], F32)],
            [("x2", [P, KT, 2 * S], F32R)])
        (uf, uu), (hid, _, rms), (bpad,), (bsq, sq_last, bmean, bsdev) = in_turn(
            "region_u", 3 * SN * S,
            [("uf", [P, SN, S], F32), ("uu", [P, SN, 2 * S], F32R)],
            [("hid", [P, 2, SN, S], F32), ("gap", [P, 3 * S], F32),
             ("rms", [P, S], F32)],
            [("bpad", [P, 4, S + 32], F32)],
            [("bsq", [P, 4, S], F32), ("sq_last", [P, S], F32), ("bmean", [P, S], F32), ("bsdev", [P, S], F32)])
        ssd = sb("ssd", [P, 2, 17, 2])
        rn = sb("rn", [P, 2, 17, 2])
        rq = sb("rq", [P, 2, 17, 2])
        gqk = sb("gqk", [P, 2])
        peak = sb("peak", [P, 3, 2, 2])
        negm = sb("negm", [P, 3, 2, 2])
        rsum = sb("rsum", [P, 3, 2, 2])
        sink = sb("sink", [P, 3, 2, 2])

        GA = ctx.enter_context(nc.psum_tensor("ps_a", [P, SN, 512], F32))
        GB = ctx.enter_context(nc.psum_tensor("ps_b", [P, SN, 512], F32))
        psum = (GA, GB)

        raw_in = [sem(f"raw_in{r}") for r in range(RING)]
        hi_done = sem("hi_done")
        lo_vec = sem("lo_vec")
        lo_pool = sem("lo_pool")
        pe_piece = sem("pe_piece")
        half_out = sem("half_out")
        strip_out = sem("strip_out")
        dve_step, pool_step = sem("dve_step"), sem("pool_step")
        params_in, const_in_sem = sem("params_in"), sem("const_in_sem")
        x_loaded = [sem(f"x_in{b}") for b in range(4)]
        const_ready = sem("const_ready")
        exp_lam = sem("exp_lam")
        xx_hi, xx_lo = sem("xx_hi"), sem("xx_lo")
        u_made, u_hi, u_lo = sem("u_made"), sem("u_hi"), sem("u_lo")
        gate_out = sem("gate_out")
        iu_ready, a_ready, sq_ready = sem("iu_ready"), sem("a_ready"), sem("sq_ready")
        tanh_ready, one_minus, root_ready = sem("tanh_ready"), sem("one_minus"), sem("root_ready")
        h_sum, h_hi, h_lo = sem("h_sum"), sem("h_hi"), sem("h_lo")
        vg_made, vg_hi, vg_lo = sem("vg_made"), sem("vg_hi"), sem("vg_lo")
        gl_sig = sem("gl_sig")
        m_made, m_hi, m_lo = sem("m_made"), sem("m_hi"), sem("m_lo")
        z_made = sem("z_made")
        ff_made, ff_hi, ff_lo, res_seed = sem("ff_made"), sem("ff_hi"), sem("ff_lo"), sem("res_seed")
        nsum, nmean, ncent, nsq, nvar, nsd, nh = (
            [sem(f"{k}{n}") for n in range(4)]
            for k in ("norm_sum", "norm_mean", "norm_centred", "norm_sq", "norm_var", "norm_sd", "norm_h"))
        bg_sum, bg_sig, b_made = sem("bg_sum"), sem("bg_sig"), sem("b_made")
        b_sum, b_mean, b_cent, b_sq, b_var, b_sd, b_norm, b_silu = (
            sem(n) for n in ("b_sum", "b_mean", "b_cent", "b_sq", "b_var", "b_sd", "b_norm", "b_silu"))
        qk_sq, qk_ssq, qk_sd, rows_ready, k_rows, k_ready = (
            sem(n) for n in ("qk_sq", "qk_ssq", "qk_sd", "rows_ready", "k_rows", "k_ready"))
        vt_psum, vt_out = sem("vt_psum"), sem("vt_out")
        score_psum, score_out, peak_ready, exp_done, rsum_ready, p_ready = (
            sem(n) for n in ("score_psum", "score_out", "peak_ready", "exp_done", "rsum_ready", "p_ready"))
        pt_psum, pt_out, o_psum = sem("pt_psum"), sem("pt_out"), sem("o_psum")
        sq_summed = sem("sq_summed")
        b_hi, b_lo = sem("b_hi"), sem("b_lo")
        rms_ready, qkv_made = sem("rms_ready"), sem("qkv_made")
        gate_sum, gate_act, gate_scaled = sem("gate_sum"), sem("gate_act"), sem("gate_scaled")
        out_done = sem("out_done")

        XX_X, XX_H1, XX_N1 = range(3)
        PAIRS = [(8 + t, 12 + t, t, 0) for t in range(4)] + [(20 + t, 28, 4, 1) for t in range(8)]
        NORMED = list(range(8, 16)) + list(range(20, 29))
        block = ctx.enter_context(nc.Block())

        @block.sync
        def _(sp):
            def quad(q, src, at, width):
                for r in range(RING):
                    sp.wait_ge(lo_vec if r % 2 == 0 else lo_pool, 2 * q - 1 + r // 2)
                    sp.dma_start(w_raw[:, r, 0:width], src[ds(at + r, 1), :, :].rearrange("a p n -> (a p) n")
                                 ).then_inc(raw_in[r], 16)

            for b in range(4):
                sp.dma_start(zz[:, 4 * b:4 * b + 4, :], x_in[:, 4 * b:4 * b + 4, :]).then_inc(x_loaded[b], 16)
                sp.dma_start(w_raw[:, b, 0:N8], w8[b, :, :]).then_inc(raw_in[b], 16)
            sp.dma_start(prm[:, :], prm_in).then_inc(params_in, 16)
            sp.dma_start(const[:, :], const_in).then_inc(const_in_sem, 16)
            for k in range(3):
                quad(1 + k, w8, 4 + 4 * k, N8)
            with sp.Fori(0, 4) as i:
                for k in range(2):
                    quad(6 * i + 4 + k, w10, 8 * i + 4 * k, N10)
                for k in range(4):
                    quad(6 * i + 6 + k, w8, 16 * i + 16 + 4 * k, N8)
            for k in range(2):
                quad(28 + k, w10, 32 + 4 * k, N10)
            with sp.Fori(0, 4) as i:
                quad(i + 30, w8, 4 * i + 80, N8)
            with sp.Fori(0, 4) as i:
                for k in range(2):
                    quad(8 * i + 34 + k, w8, 24 * i + 96 + 4 * k, N8)
                for k in range(2):
                    quad(8 * i + 36 + k, w10, 8 * i + 40 + 4 * k, N10)
                for k in range(4):
                    quad(8 * i + 38 + k, w8, 24 * i + 104 + 4 * k, N8)
            with sp.Fori(0, 161) as i:
                quad(i + 66, w8, 4 * i + 192, N8)
            for j in range(4):
                sp.wait_ge(strip_out, outs(160 + j))
                sp.dma_start(out[:, 4 * j:4 * j + 4, :], res[:, 4 * j:4 * j + 4, :]).then_inc(out_done, 16)
            sp.wait_ge(out_done, 64)

        @block.tensor
        def _(pe):
            def piece_ready(q, r):
                pe.wait_ge(hi_done, 4 * q + r + 1)
                pe.wait_ge(lo_vec if r % 2 == 0 else lo_pool, 2 * q + 1 + r // 2)

            def strip(q, e, group, src, kt, need, per=8, gates_of=None, gates_in=None, nout=SN, free=None,
                      free_last=None, r0=0, ks=None, at=0):
                tiles = [(k, j) for k in ks or range(kt) for j in range(nout)]
                main = per if gates_of is None else per - 2
                if free is not None:
                    free()
                for p, first in enumerate(range(0, len(tiles), main)):
                    r = (p + r0) % 4
                    piece_ready(q + (p + r0) // 4, r)
                    for o, (k, j) in enumerate(tiles[first:first + main]):
                        cols = slice(o * P, o * P + P)
                        if j == 0:
                            need(k)
                        if k == 0 and j == SN - 1 and free_last is not None:
                            free_last()
                        nc.tensor.matmul(group[:, j, :], w_hi[:, r, cols], src[:, at + k, :], start=k == 0, stop=False)
                        last = nc.tensor.matmul(group[:, j, 0:S], w_lo[:, r, cols], src[:, at + k, 0:S],
                                                start=False, stop=k == kt - 1)
                    if gates_of is not None:
                        last = gate_pair(gates_of, e, gates_in, p, r)
                    last.then_inc(pe_piece, 1)

            def gate_pair(s, e, group, g, r):
                if g == 0:
                    pe.wait_ge(u_hi, s)
                    pe.wait_ge(u_lo, s)
                    pe.wait_ge(strip_out, outs(e))
                if g >= 4:
                    pe.wait_ge(gate_out, 8 * s + g - 11)
                for kind in range(2):
                    cols = slice((8 + kind) * P, (9 + kind) * P)
                    dst, hd = group[:, g % 4, kind * S:kind * S + S], g // 2
                    nc.tensor.matmul(dst, w_hi[:, r, cols], uu[:, hd, 0:S], start=True, stop=False)
                    nc.tensor.matmul(dst, w_hi[:, r, cols], uu[:, hd, S:2 * S], start=False, stop=False)
                    last = nc.tensor.matmul(dst, w_lo[:, r, cols], uu[:, hd, 0:S], start=False, stop=True)
                return last

            def need_x(version):
                def need(k):
                    if k % 4 == 0:
                        pe.wait_ge(xx_hi, 4 * version + k // 4 + 1)
                        pe.wait_ge(xx_lo, 4 * version + k // 4 + 1)
                return need

            def nothing(k):
                pass

            def out_before(e):
                return lambda: pe.wait_ge(strip_out, outs(e - 1))

            def three(s, q, e, odd):
                main, other = (GA, GB) if odd else (GB, GA)
                strip(q, e, main, xx, KT, nothing, per=10, gates_of=s, gates_in=other, free=out_before(e))
                strip(q + 2, e + 1, other, xx, KT, nothing, free=lambda: pe.wait_ge(gate_out, 8 * s - 1),
                      free_last=lambda: pe.wait_ge(gate_out, 8 * s))
                strip(q + 4, e + 2, main, xx, KT, nothing, free=out_before(e + 2))

            strip(0, 0, GB, xx, KT, need_x(XX_X))
            strip(2, 1, GA, xx, KT, nothing)
            with pe.Fori(0, 2) as i:
                for k in range(2):
                    three(2 * i + k + 1, 12 * i + 6 * k + 4, 6 * i + 3 * k + 2, k == 1)
            three(5, 28, 14, False)
            def need_h(k):
                if k == 0:
                    pe.wait_ge(h_hi, 5)
                    pe.wait_ge(h_lo, 6)

            def need_v(k):
                if k % 4 == 0:
                    pe.wait_ge(vg_hi, k // 4 + 1)
                    pe.wait_ge(vg_lo, k // 4 + 1)

            with pe.Fori(0, 4) as i:
                q, e = 8 * i + 34, 4 * i + 17
                strip(q, e, GA, xx, KT, nothing, free=out_before(e))
                strip(q + 2, e + 1, GB, hh, HT, need_h, per=10, free=out_before(e + 1))
                strip(q + 4, e + 2, GA, xx, KT, nothing, free=out_before(e + 2))
                strip(q + 6, e + 3, GB, vv, KT, need_v, free=out_before(e + 3))

            def need_m(k):
                if k % 4 == 0:
                    pe.wait_ge(m_hi, k // 4 + 1)
                    pe.wait_ge(m_lo, k // 4 + 1)

            with pe.Fori(0, 2) as i:
                strip(4 * i + 66, 2 * i + 33, GA, mx, KT, need_m, free=out_before(2 * i + 33))
                strip(4 * i + 68, 2 * i + 34, GB, mx, KT, need_m, free=out_before(2 * i + 34))

            def column_sums(src, ready, done, bank, tiles=KT):
                for k in range(tiles):
                    if k % 4 == 0:
                        ready(k // 4)
                    last = nc.tensor.matmul(bank, ones[:, :], src[:, k, :], start=k == 0, stop=k == tiles - 1)
                last.then_inc(done, 1)

            pe.wait_ge(const_ready, 1)
            pe.wait_ge(strip_out, outs(36))
            column_sums(zz, lambda b: pe.wait_ge(z_made, b + 1), nsum[0], GA[:, 0, 0:S])
            column_sums(squares, lambda b: pe.wait_ge(nsq[0], b + 1), nvar[0], GA[:, 1, 0:S])

            def need_ff(before):
                def need(k):
                    if k % 4 == 0:
                        pe.wait_ge(ff_hi, before + k // 4 + 1)
                        pe.wait_ge(ff_lo, before + k // 4 + 1)
                return need

            with pe.Fori(0, 8) as i:
                q, e = 8 * i + 74, 6 * i + 37
                strip(q, e, GA, xx, KT, need_x(XX_H1), free=out_before(e))
                strip(q + 2, e + 1, GB, xx, KT, nothing, free=out_before(e + 1))
                for p in range(0, 4, 2):
                    for ks in (range(0, 4), range(4, 8)):
                        for j in range(2):
                            strip(q + 4 + p + ks[0] // 4, e + 2 + p + j, psum[j], ff, 8, need_ff(2 * i), r0=2 * j, ks=ks,
                                  free=out_before(e + 2 + p + j) if ks[0] == 0 else None)
            pe.wait_ge(strip_out, outs(84))
            column_sums(res, lambda b: pe.wait_ge(strip_out, outs(82 + b)), nsum[1], GA[:, 0, 0:S])
            column_sums(squares, lambda b: pe.wait_ge(nsq[1], b + 1), nvar[1], GA[:, 1, 0:S])

            def rms_beside(n, need):
                def need_and_sum(k):
                    need(k)
                    if k == 12:
                        column_sums(squares, lambda b: pe.wait_ge(sq_summed, n - 1), nvar[n], GB[:, 1, 0:S], 4)
                return need_and_sum

            strip(138, 85, GA, xx, KT, rms_beside(2, need_x(XX_N1)), free=out_before(85))
            strip(140, 86, GB, xx, KT, nothing, free=lambda: pe.wait_ge(nsd[2], 1))
            with pe.Fori(0, 2) as i:
                strip(4 * i + 142, 2 * i + 87, GA, xx, KT, nothing, free=out_before(2 * i + 87))
                strip(4 * i + 144, 2 * i + 88, GB, xx, KT, nothing, free=out_before(2 * i + 88))
            strip(150, 91, GA, xx, KT, nothing, free=out_before(91))
            strip(152, 92, GB, xx, KT, nothing, nout=2, free=out_before(92))
            pe.wait_ge(const_in_sem, 16)

            def head_sums(n, src):
                for blk in range(2):
                    last = nc.tensor.matmul(GB[:, 3, (blk * 17 + n) * 2:(blk * 17 + n) * 2 + 2],
                                            src[:, blk * P:blk * P + P], pair_ones, start=True, stop=True)
                return last

            def values_by_token(n, tile):
                for blk in range(2):
                    m = blk * 5 + n
                    last = nc.tensor.transpose(GA[:, m // 4, (m % 4) * P:(m % 4) * P + P],
                                               qkv[:, tile, blk * P:blk * P + P], ident)
                return last

            for n in range(16):
                if n % 8 == 0:
                    pe.wait_ge(qk_sq, n // 8 + 1)
                head_sums(n, squares[:, n, :])
            pe.wait_ge(strip_out, outs(92))
            for n in range(4):
                values_by_token(n, 16 + n)
            pe.wait_ge(qk_sq, 3)
            head_sums(16, sq_last).then_inc(qk_ssq, 1)
            pe.wait_ge(qkv_made, 8)
            values_by_token(4, 29).then_inc(vt_psum, 1)
            column_sums(bconv, lambda b: pe.wait_ge(b_made, 4), b_sum, GA[:, 3, 0:S], 4)
            pe.wait_ge(rows_ready, 1)
            for n in range(5):
                for blk in range(2):
                    last = nc.tensor.matmul(GB[:, n // 2, (n % 2) * S + blk * P:(n % 2) * S + blk * P + P],
                                            rn_rows[:, blk, n, :], ident, start=True, stop=True)
            last.then_inc(k_rows, 1)
            column_sums(bsq, lambda b: pe.wait_ge(b_sq, 1), b_var, GA[:, 3, S:2 * S], 4)

            def scores(n):
                qt, kt_, _, _ = PAIRS[n]
                if n == 0:
                    pe.wait_ge(vt_out, 1)
                    pe.wait_ge(k_ready, 1)
                if n == 1:
                    pe.wait_ge(b_sd, 1)
                if n >= 2:
                    pe.wait_ge(score_out, n - 1)
                for hd in range(2):
                    part = slice(64 * hd, 64 * hd + 64)
                    bank = GA[:, 2 * (n % 2) + hd, :]
                    nc.tensor.matmul(bank[:, 0:P], qkv[part, qt, 0:P], qkv[part, kt_, 0:P], start=True, stop=True)
                    last = nc.tensor.matmul(bank[:, P:3 * P], qkv[part, qt, P:S], qkv[part, kt_, 0:S],
                                            start=True, stop=True)
                last.then_inc(score_psum, 1)

            def transposes(n):
                pe.wait_ge(p_ready, n + 1)
                if n >= 1:
                    pe.wait_ge(pt_out, n)
                for hd in range(2):
                    for c in range(3):
                        cols = slice(c * P, c * P + P)
                        last = nc.tensor.transpose(GB[:, hd, cols], probs[:, n % 3, hd, cols], ident)
                last.then_inc(pt_psum, 1)

            def values(n):
                v = PAIRS[n][2]
                pe.wait_ge(pt_out, n + 1)
                if n >= 2:
                    pe.wait_ge(xx_lo, 12 + n - 1)
                for hd in range(2):
                    part = slice(64 * hd, 64 * hd + 64)
                    bank = GB[part, 2 + n % 2, :]
                    nc.tensor.matmul(bank[:, 0:S], vt[:, 0, v, part], probs_t[:, n % 2, hd, 0:S], start=True, stop=False)
                    last = nc.tensor.matmul(bank[:, P:S], vt[:, 1, v, part], probs_t[:, n % 2, hd, 2 * P:3 * P],
                                            start=False, stop=True)
                last.then_inc(o_psum, 1)

            scores(0)
            scores(1)
            for n in range(12):
                if n < 10:
                    scores(n + 2)
                if n >= 1:
                    values(n - 1)
                transposes(n)
            values(11)
            def need_mix(k):
                if k == 0:
                    pe.wait_ge(xx_hi, 24)
                    pe.wait_ge(xx_lo, 24)
                    pe.wait_ge(b_hi, 1)
                    pe.wait_ge(b_lo, 1)

            with pe.Fori(0, 2) as i:
                strip(4 * i + 153, 2 * i + 93, GA, xx, KT, need_mix, free=out_before(2 * i + 93))
                strip(4 * i + 155, 2 * i + 94, GB, xx, KT, nothing, free=out_before(2 * i + 94))
            def need_n2(k):
                if k % 4 == 0:
                    pe.wait_ge(xx_hi, 24 + k // 4 + 1)
                    pe.wait_ge(xx_lo, 24 + k // 4 + 1)

            def down(q, e, n, first, tiles=range(4)):
                for j in range(4):
                    strip(q + j // 2, e + j, psum[(j + first) % 2], ff, 4, need_ff(n + 16), free=out_before(e + j),
                          r0=2 * (j % 2), at=tiles[0])

            def need_n2_and_bank(k):
                need_n2(k)
                if k == 12:
                    pe.wait_ge(strip_out, outs(97))

            strip(161, 97, GA, x2, KT, rms_beside(3, need_n2_and_bank), free=out_before(97))
            strip(163, 98, GB, x2, KT, nothing, free=lambda: pe.wait_ge(nsd[3], 1))
            with pe.Fori(0, 9) as i:
                q, e = 6 * i + 165, 6 * i + 99
                strip(q, e, GA, x2, KT, nothing, free=out_before(e))
                down(q + 2, e + 1, i, 1)
                strip(q + 4, e + 5, GB, x2, KT, nothing, free=out_before(e + 5))
            strip(219, 153, GA, x2, KT, nothing, free=out_before(153))
            strip(221, 154, GB, x2, KT, nothing, free=out_before(154))
            down(223, 155, 9, 0)
            down(225, 159, 10, 0, range(4, 8))

        @block.scalar
        def _(act):
            def split(q, r, width=N8):
                act.wait_ge(raw_in[r], 16 * q + 16)
                if not (isinstance(q, int) and q == 0):
                    act.wait_ge(pe_piece, 4 * q + r - 3)
                act.activation(w_hi[:, r, 0:width], w_raw[:, r, 0:width], ACT.Copy).then_inc(hi_done, 1)

            def splits(q, width=N8, slots=range(RING)):
                for r in slots:
                    split(q, r, width)

            def halves(e, pieces, group, nout=SN):
                act.wait_ge(pe_piece, pieces)
                if not (isinstance(e, int) and e == 0):
                    act.wait_ge(strip_out, outs(e))
                act.activation(half[:, 0:nout, :], group[:, 0:nout, S:2 * S], ACT.Copy).then_inc(half_out, 1)

            def hi_of(dst, src, made, n, done):
                act.wait_ge(made, n)
                act.activation(dst, src, ACT.Copy).then_inc(done, 1)

            for b in range(4):
                split(0, b)
                act.wait_ge(x_loaded[b], 16)
                act.activation(xx[:, 4 * b:4 * b + 4, 0:S], zz[:, 4 * b:4 * b + 4, :], ACT.Copy).then_inc(xx_hi, 1)
            splits(1)
            act.wait_ge(const_ready, 2)
            act.activation(decay[:, :], decay[:, :], ACT.Exp, scale=-1.0).then_inc(exp_lam, 1)
            splits(2)
            halves(0, 8, GB)
            splits(3)
            hi_of(uu[:, :, 0:S], uf[:, :, :], u_made, 1, u_hi)
            splits(4, N10)
            halves(1, 16, GA)

            def of_r(dst, s, function):
                for hd in range(SN):
                    for way in range(2):
                        c = way * HT + hd - 4 + 4 * s
                        last = act.activation(dst[:, way, hd, :], gates[:, hd, way, 0, :], function,
                                              scale=decay[:, ds(c, 1)])
                return last

            def three(s, q, e, odd, conv, wide):
                main, other = (GA, GB) if odd else (GB, GA)
                act.wait_ge(h_lo, s)
                for g in range(8):
                    split(q + 1 + g // 4, g % 4, N10 if g < 4 else N8)
                    act.wait_ge(pe_piece, 4 * q + g + 1)
                    hd, way = g // 2, g % 2
                    for kind, name in enumerate(("b_a", "b_x")):
                        last = act.activation(gates[:, hd, way, kind, :], other[:, g % 4, kind * S:kind * S + S],
                                              ACT.Sigmoid, bias=prm[:, ds(COL[name] + way * HT + hd - 4 + 4 * s, 1)])
                    last.then_inc(gate_out, 1)
                halves(e, 4 * q + 8, main)
                split(q + 3, 0)
                of_r(aa, s, ACT.Exp).then_inc(a_ready, 1)
                split(q + 3, 1)
                split(q + 3, 2)
                of_r(tt, s, ACT.Tanh).then_inc(tanh_ready, 1)
                split(q + 3, 3)
                split(q + 4, 0)
                if conv:
                    hi_of(uu[:, :, 0:S], uf[:, :, :], u_made, s + 1, u_hi)
                splits(q + 4, N8, (1, 2, 3))
                halves(e + 1, 4 * q + 16, other)
                split(q + 5, 0)
                act.wait_ge(one_minus, s)
                act.activation(tt[:, :, :, :], tt[:, :, :, :], ACT.Sqrt, scale=-1.0).then_inc(root_ready, 1)
                splits(q + 5, N8, (1, 2, 3))
                splits(q + 6, wide, (0, 1, 2))
                hi_of(hh[:, ds(4 * s - 4, 4), 0:S], gates[:, :, 0, 0, :], h_sum, s, h_hi)
                split(q + 6, 3, wide)
                halves(e + 2, 4 * q + 24, main)

            with act.Fori(0, 2) as i:
                for k in range(2):
                    three(2 * i + k + 1, 12 * i + 6 * k + 4, 6 * i + 3 * k + 2, k == 1, True, N10)
            three(5, 28, 14, False, False, N8)

            def v_hi(b):
                if b == 0:
                    act.wait_ge(h_lo, 6)
                hi_of(vv[:, 4 * b:4 * b + 4, 0:S], v32[:, 4 * b:4 * b + 4, :], vg_made, min(b + 1, 3), vg_hi)

            def plain(q, e, group, nout=SN):
                splits(q + 1)
                splits(q + 2)
                halves(e, 4 * q + 8, group, nout)

            for b in range(4):
                v_hi(b)
            with act.Fori(0, 4) as i:
                q, e = 8 * i + 34, 4 * i + 17
                for k in range(4):
                    splits(q + 2 * k + 1, N10 if k == 1 else N8)
                    splits(q + 2 * k + 2, N10 if k == 0 else N8)
                    halves(e + k, 4 * (q + 2 * k) + 8, psum[k % 2])
                    if k % 2 == 0:
                        act.wait_ge(strip_out, outs(e + k + 1))
                        act.activation(hid[:, 0, :, :], hid[:, 0, :, :], ACT.Sigmoid).then_inc(gl_sig, 1)
            for b in range(4):
                hi_of(mx[:, 4 * b:4 * b + 4, 0:S], m32[:, 4 * b:4 * b + 4, :], m_made, b + 1, m_hi)
            with act.Fori(0, 2) as i:
                plain(4 * i + 66, 2 * i + 33, GA)
                plain(4 * i + 68, 2 * i + 34, GB)

            def norm(n, src, base):
                act.activation(warm[:, n:n + 1], eps[:, 0:1], ACT.Sqrt)
                act.wait_ge(nsum[n], 1)
                act.activation(mean[:, :], GA[:, 0, 0:S], ACT.Copy, scale=1.0 / D).then_inc(nmean[n], 1)
                for b in range(4):
                    act.wait_ge(ncent[n], b + 1)
                    act.activation(squares[:, 4 * b:4 * b + 4, :], src[:, 4 * b:4 * b + 4, :],
                                   ACT.Square).then_inc(nsq[n], 1)
                act.wait_ge(nvar[n], 1)
                act.activation(sdev[:, :], GA[:, 1, 0:S], ACT.Sqrt, scale=1.0 / D, bias=eps[:, 0:1]).then_inc(nsd[n], 1)
                if base is not None:
                    for b in range(4):
                        hi_of(xx[:, 4 * b:4 * b + 4, 0:S], hnorm[:, b % 2, :, :], nh[n], b + 1, xx_hi)

            def gained_hi(dst, b, gain):
                for j in range(SN):
                    last = act.activation(dst[:, ds(4 * b + j, 1), 0:S], res[:, ds(4 * b + j, 1), :], ACT.Copy,
                                          scale=prm[:, ds(COL[gain] + j + 4 * b, 1)])
                last.then_inc(xx_hi, 1)

            def res_square(n, b):
                act.activation(squares[:, ds(4 * b, 4), :], res[:, ds(4 * b, 4), :], ACT.Square).then_inc(nsq[n], 1)

            def rms_root(n):
                act.wait_ge(nvar[n], 1)
                act.activation(rms[:, :], GB[:, 1, 0:S], ACT.Sqrt, scale=1.0 / D, bias=eps[:, 1:2]).then_inc(nsd[n], 1)

            norm(0, zz, 4)
            with act.Fori(0, 8) as i:
                q, e = 8 * i + 74, 6 * i + 37
                for k in range(2):
                    plain(q + 2 * k, e + k, psum[k])
                    hi_of(ff[:, 4 * k:4 * k + 4, 0:S], hid[:, k, :, :], ff_made, 2 * i + k + 1, ff_hi)
                for p in range(0, 4, 2):
                    splits(q + p + 5)
                    splits(q + p + 6, N8, (0, 1))
                    halves(e + 2 + p, 4 * (q + p + 5) + 2, GA)
                    splits(q + p + 6, N8, (2, 3))
                    halves(e + 3 + p, 4 * (q + p + 5) + 4, GB)
            norm(1, res, None)
            for b in range(4):
                act.wait_ge(nh[1], b + 1)
                gained_hi(xx, b, "n1_g")
                res_square(2, b)
            splits(139)
            splits(140, N8, (0, 1))
            rms_root(2)
            splits(140, N8, (2, 3))
            halves(85, 4 * 140, GA)
            plain(140, 86, GB)
            act.wait_ge(qkv_made, 2)
            act.activation(qkv[:, 4:8, :], qkv[:, 4:8, :], ACT.Sigmoid).then_inc(bg_sig, 1)
            with act.Fori(0, 2) as i:
                for k in range(2):
                    plain(4 * i + 2 * k + 142, 2 * i + k + 87, psum[k])
            act.wait_ge(qkv_made, 4)
            act.activation(squares[:, 0:8, :], qkv[:, 8:16, :], ACT.Square).then_inc(qk_sq, 1)
            plain(150, 91, GA)
            splits(153)
            act.wait_ge(qkv_made, 7)
            act.activation(squares[:, 8:16, :], qkv[:, 20:28, :], ACT.Square).then_inc(qk_sq, 1)
            halves(92, 4 * 153, GB, 2)
            act.wait_ge(qkv_made, 8)
            act.wait_ge(b_made, 4)
            act.activation(sq_last[:, :], qkv[:, 28, :], ACT.Square).then_inc(qk_sq, 1)
            act.wait_ge(qk_ssq, 1)
            act.activation(ssd[:, :, :, :].rearrange("p b n h -> p (b n h)"), GB[:, 3, 0:68], ACT.Sqrt,
                           scale=1.0 / HD, bias=eps[:, 1:2]).then_inc(qk_sd, 1)
            act.wait_ge(b_sum, 1)
            act.activation(bmean[:, :], GA[:, 3, 0:S], ACT.Copy, scale=1.0 / (4 * P)).then_inc(b_mean, 1)
            act.wait_ge(b_cent, 1)
            act.activation(bsq[:, :, :], bconv[:, :, :], ACT.Square).then_inc(b_sq, 1)
            act.wait_ge(vt_psum, 1)
            vt_rows = vt[:, :, :, :].rearrange("p b n c -> p (b n c)")
            act.activation(vt_rows[:, 0:1024].rearrange("p (b c) -> p b c", b=2), GA[:, 0:2, :], ACT.Copy)
            act.activation(vt_rows[:, 1024:1280], GA[:, 2, 0:S], ACT.Copy).then_inc(vt_out, 1)
            act.wait_ge(b_var, 1)
            act.activation(bsdev[:, :], GA[:, 3, S:2 * S], ACT.Sqrt, scale=1.0 / (4 * P), bias=eps[:, 1:2]
                           ).then_inc(b_sd, 1)

            def exps(n):
                act.wait_ge(peak_ready, n + 1)
                b = n % 3
                for hd in range(2):
                    for blk, cols in ((0, slice(0, P)), (1, slice(P, 3 * P))):
                        last = act.activation(probs[:, b, hd, cols], probs[:, b, hd, cols], ACT.Exp,
                                              bias=negm[:, b, hd, blk:blk + 1], accum_out=rsum[:, b, hd, blk:blk + 1])
                if PAIRS[n][3]:
                    for hd in range(2):
                        c = COL["sinks"] + n - 4 + 8 * hd
                        last = act.activation(sink[:, b, hd, :], negm[:, b, hd, :], ACT.Exp, bias=prm[:, c:c + 1])
                last.then_inc(exp_done, 1)

            exps(0)
            exps(1)
            for n in range(13):
                if n >= 1:
                    act.wait_ge(o_psum, n)
                    act.activation(xx[:, mix_tile(n - 1), 0:S], GB[:, 2 + (n - 1) % 2, 0:S], ACT.Copy).then_inc(xx_hi, 1)
                if n < 12:
                    act.wait_ge(pt_psum, n + 1)
                    if n >= 2:
                        act.wait_ge(o_psum, n - 1)
                    act.activation(probs_t[:, n % 2, :, :], GB[:, 0:2, 0:3 * P], ACT.Copy).then_inc(pt_out, 1)
                if n < 10:
                    exps(n + 2)
                if n == 3:
                    act.wait_ge(b_norm, 1)
                    act.activation(bconv[:, :, :], bconv[:, :, :], ACT.Silu).then_inc(b_silu, 1)
                    hi_of(xx[:, 4:8, 0:S], bconv[:, :, :], b_silu, 1, b_hi)
            with act.Fori(0, 2) as i:
                for k in range(2):
                    plain(4 * i + 2 * k + 153, 2 * i + k + 93, psum[k])
                    act.wait_ge(strip_out, outs(2 * i + k + 94))
                    gained_hi(x2, 2 * i + k, "n2_g")
                    res_square(3, 2 * i + k)

            def silu(n):
                act.wait_ge(gate_sum, n + 1)
                act.activation(hid[:, 0, :, :], hid[:, 0, :, :], ACT.Silu).then_inc(gate_act, 1)

            def ff_hi_of(n, at=0):
                hi_of(ff[:, at:at + 4, 0:S], hid[:, 1, :, :], ff_made, 17 + n, ff_hi)

            splits(162)
            splits(163, N8, (0, 1))
            rms_root(3)
            splits(163, N8, (2, 3))
            halves(97, 4 * 163, GA)
            split(164, 0)
            silu(0)
            splits(164, N8, (1, 2, 3))
            splits(165)
            halves(98, 4 * 165, GB)
            ff_hi_of(0)
            def downs(q, e, first, j):
                splits(q + 1 + j // 2, N8, (0, 1) if j % 2 == 0 else (2, 3))
                halves(e + j, 4 * q + 2 * j + 2, psum[(j + first) % 2])

            with act.Fori(0, 9) as i:
                q, e = 6 * i + 165, 6 * i + 99
                plain(q, e, GA)
                for j in range(4):
                    downs(q + 2, e + 1, 1, j)
                    if j == 0:
                        silu(i + 1)
                plain(q + 4, e + 5, GB)
                ff_hi_of(i + 1)
            plain(219, 153, GA)
            split(222, 0)
            silu(10)
            splits(222, N8, (1, 2, 3))
            splits(223)
            halves(154, 4 * 223, GB)
            downs(223, 155, 0, 0)
            ff_hi_of(10, 4)
            for j in range(1, 4):
                downs(223, 155, 0, j)
            for j in range(2):
                downs(225, 159, 0, j)
            for j in range(2, 4):
                halves(159 + j, 4 * 225 + 2 * j + 2, psum[j % 2])

        @block.vector
        def _(dve):
            own = Steps(dve, dve_step)

            def lo(q, r, width=N8):
                dve.wait_ge(hi_done, 4 * q + r + 1)
                if not (isinstance(q, int) and q == 0):
                    dve.wait_ge(pe_piece, 4 * q + r - 3)
                dve.tensor_tensor(w_lo[:, r, 0:width], w_raw[:, r, 0:width], w_hi[:, r, 0:width].bitcast(F32),
                                  ALU.subtract).then_inc(lo_vec, 1)

            def los(q, width=N8, slots=(0, 2)):
                for r in slots:
                    lo(q, r, width)

            def total(e, group, dst, nout=SN):
                dve.wait_ge(half_out, e + 1)
                dve.tensor_tensor(dst, group[:, 0:nout, 0:S], half[:, 0:nout, :], ALU.add).then_inc(strip_out, 1)
                dve.wait_ge(strip_out, outs(e + 1))

            def add_total(e, group, dst):
                dve.wait_ge(half_out, e + 1)
                own.done(dve.tensor_tensor(dst, group[:, :, 0:S], dst, ALU.add))
                own.need()
                dve.tensor_tensor(dst, half[:, :, :], dst, ALU.add).then_inc(strip_out, 1)

            def lo_of(dst, src, hi, n, hi_sem, done):
                dve.wait_ge(hi_sem, n)
                dve.tensor_tensor(dst, src, hi.bitcast(F32), ALU.subtract).then_inc(done, 1)

            def column(name, n):
                return prm[:, ds(COL[name] + n, 1)]

            dve.memset(eps[:, 0:1], LN_EPS)
            dve.memset(eps[:, 1:2], RMS_EPS)
            dve.memset(padded[:, :, :], 0.0).then_inc(strip_out, 1)
            dve.memset(ones[:, :], 1.0).then_inc(const_ready, 1)
            for b in range(4):
                if b % 2 == 0:
                    lo(0, b)
                lo_of(xx[:, 4 * b:4 * b + 4, S:2 * S], zz[:, 4 * b:4 * b + 4, :], xx[:, 4 * b:4 * b + 4, 0:S],
                      b + 1, xx_hi, xx_lo)
            los(1)
            lam = prm[:, COL["lam"]:COL["lam"] + 2 * HT]
            neg, sq, poly = series[:, 0, :], series[:, 1, :], series[:, 2, :]
            dve.wait_ge(params_in, 16)
            own.done(dve.tensor_scalar(neg, lam, -1.0, None, ALU.mult))
            own.need()
            dve.tensor_tensor(decay[:, :], lam, neg, ALU.max).then_inc(const_ready, 1)
            own.done(dve.tensor_scalar(neg, neg, 0.0, None, ALU.max))
            dve.wait_ge(exp_lam, 1)
            own.done(dve.tensor_scalar(sq, decay[:, :], 2.0, None, ALU.add))
            own.need()
            own.done(dve.reciprocal(poly, sq))
            own.need()
            own.done(dve.tensor_tensor(decay[:, :], decay[:, :], poly, ALU.mult))
            own.need()
            own.done(dve.tensor_tensor(sq, decay[:, :], decay[:, :], ALU.mult))
            own.need()
            own.done(dve.tensor_scalar(poly, sq, 1.0 / 17, 1.0 / 15, ALU.mult, ALU.add))
            for odd in (13, 11, 9, 7, 5, 3, 1):
                own.need()
                own.done(dve.tensor_tensor(poly, poly, sq, ALU.mult))
                own.need()
                own.done(dve.tensor_scalar(poly, poly, 1.0 / odd, None, ALU.add))
            own.need()
            own.done(dve.tensor_tensor(poly, poly, decay[:, :], ALU.mult))
            own.need()
            own.done(dve.scalar_tensor_tensor(poly, poly, 2.0, neg, ALU.mult, ALU.add))
            own.need()
            own.done(dve.tensor_scalar(decay[:, :], poly, -LRU_C, None, ALU.mult))
            own.done(dve.tensor_tensor(gqk[:, 0:1], column("aq_g", 0), column("ak_g", 0), ALU.mult))
            own.done(dve.tensor_tensor(gqk[:, 1:2], column("cq_g", 0), column("ck_g", 0), ALU.mult))
            dve.memset(sink[:, :, :, :], 0.0).then_inc(h_lo, 1)
            los(2)

            def conv_u(s):
                taps = []
                for hd in range(SN):
                    taps.append(own.done(dve.tensor_scalar(
                        uf[:, hd, :], padded[:, hd, 0:S], column("lru_w", hd + 4 * s), column("lru_b", hd + 4 * s),
                        ALU.mult, ALU.add)))
                for k in range(1, 4):
                    for hd in range(SN):
                        own.need(taps[hd])
                        ins = dve.scalar_tensor_tensor(
                            uf[:, hd, :], padded[:, hd, k:k + S], column("lru_w", k * HT + hd + 4 * s),
                            uf[:, hd, :], ALU.mult, ALU.add)
                        if k == 3 and hd == SN - 1:
                            ins.then_inc(u_made, 1)
                        else:
                            taps[hd] = own.done(ins)

            def conv_v(b):
                taps = []
                for j in range(SN):
                    taps.append(own.done(dve.tensor_scalar(
                        v32[:, ds(4 * b + j, 1), :], padded[:, j:j + 1, 1:1 + S], column("sc_w", j + 4 * b),
                        column("sc_b", j + 4 * b), ALU.mult, ALU.add)))
                for k in range(1, 3):
                    for j in range(SN):
                        own.need(taps[j])
                        taps[j] = own.done(dve.scalar_tensor_tensor(
                            v32[:, ds(4 * b + j, 1), :], padded[:, j:j + 1, k + 1:k + 1 + S],
                            column("sc_w", k * KT + j + 4 * b), v32[:, ds(4 * b + j, 1), :], ALU.mult, ALU.add))

            def times(e, group, dst, vg=True):
                dve.wait_ge(half_out, e + 1)
                dve.tensor_tensor(half[:, :, :], group[:, :, 0:S], half[:, :, :], ALU.add).then_inc(strip_out, 1)
                dve.wait_ge(strip_out, outs(e + 1))
                product = dve.tensor_tensor(dst, dst, half[:, :, :], ALU.mult)
                if vg:
                    product.then_inc(vg_made, 1)
                else:
                    own.done(product)

            total(0, GB, padded[:, :, 2:2 + S])
            conv_u(0)
            lo(3, 0)
            lo_of(uu[:, :, S:2 * S], uf[:, :, :], uu[:, :, 0:S], 1, u_hi, u_lo)
            lo(3, 2)
            los(4, N10)
            total(1, GA, b3[:, :, :])
            lo(5, 0, N10)

            def three(s, q, e, odd, last_heads):
                main, other = (GA, GB) if odd else (GB, GA)
                lo(q + 1, 2, N10)
                los(q + 2)
                if last_heads:
                    times(e, main, v32[:, 0:4, :])
                else:
                    own.need()
                    total(e, main, padded[:, :, 2:2 + S])
                lo(q + 3, 0)
                if not last_heads:
                    dve.wait_ge(iu_ready, 2 * s)
                    conv_u(s)
                lo(q + 3, 2)
                if not last_heads:
                    lo_of(uu[:, :, S:2 * S], uf[:, :, :], uu[:, :, 0:S], s + 1, u_hi, u_lo)
                lo(q + 4, 0)
                dve.wait_ge(sq_ready, s)
                dve.wait_ge(tanh_ready, s)
                for way in range(2):
                    last = dve.scalar_tensor_tensor(tt[:, way, :, :], gates[:, :, way, 0, :], 1.0, tt[:, way, :, :],
                                                    ALU.add, ALU.mult)
                last.then_inc(one_minus, 1)
                lo(q + 4, 2)
                if last_heads:
                    times(e + 1, other, v32[:, 4:8, :])
                else:
                    total(e + 1, other, padded[:, :, 2:2 + S])
                lo(q + 5, 0)
                dve.wait_ge(root_ready, s)
                dve.wait_ge(iu_ready, 2 * s)
                gx = [own.done(dve.tensor_tensor(tt[:, way, :, :], tt[:, way, :, :], gates[:, :, way, 1, :], ALU.mult))
                      for way in range(2)]
                for way, order in ((0, slice(None)), (1, slice(None, None, -1))):
                    own.need(gx[way])
                    for hd in range(SN):
                        own.done(dve.tensor_tensor_scan(gates[:, hd, way, 0, order], aa[:, way, hd, order],
                                                        tt[:, way, hd, order], 0.0, ALU.mult, ALU.add))
                    lo(*((q + 5, 2) if way == 0 else (q + 6, 0)), N8 if way == 0 or last_heads else N10)
                own.need()
                dve.tensor_tensor(gates[:, :, 0, 0, :], gates[:, :, 0, 0, :], gates[:, :, 1, 0, :],
                                  ALU.add).then_inc(h_sum, 1)
                blocks = ds(4 * s - 4, 4)
                lo(q + 6, 2, N8 if last_heads else N10)
                lo_of(hh[:, blocks, S:2 * S], gates[:, :, 0, 0, :], hh[:, blocks, 0:S], s, h_hi, h_lo)
                if last_heads:
                    times(e + 2, main, v32[:, 8:12, :])
                else:
                    times(e + 2, main, padded[:, :, 2:2 + S], vg=False)
                    lo(q + 7, 0, N10)
                    own.need()
                    conv_v(s - 1)

            with dve.Fori(0, 2) as i:
                own.enter(i, 2 * (15 + 10 + 1 + 12))
                for k in range(2):
                    three(2 * i + k + 1, 12 * i + 6 * k + 4, 6 * i + 3 * k + 2, k == 1, False)
                own.leave(2)
            own.need()
            own.done(dve.tensor_tensor(v32[:, 12:16, :], v32[:, 12:16, :], b3[:, :, :], ALU.mult))
            three(5, 28, 14, False, True)

            def plain(q, e, group, dst, nout=SN):
                los(q + 1)
                los(q + 2)
                total(e, group, dst, nout)

            def v_lo(b):
                lo_of(vv[:, 4 * b:4 * b + 4, S:2 * S], v32[:, 4 * b:4 * b + 4, :], vv[:, 4 * b:4 * b + 4, 0:S],
                      b + 1, vg_hi, vg_lo)

            for b in range(4):
                v_lo(b)
            def merge(i, q, e, after_total=None):
                block_ = m32[:, ds(4 * i, 4), :]
                for k in range(4):
                    los(q + 2 * k + 1, N10 if k == 1 else N8)
                    los(q + 2 * k + 2, N10 if k == 0 else N8)
                    total(e + k, psum[k % 2], hid[:, k % 2, :, :])
                    if k == 1:
                        dve.wait_ge(gl_sig, 2 * i + 1)
                        own.done(dve.tensor_tensor(block_, hid[:, 0, :, :], hid[:, 1, :, :], ALU.mult))
                    if k == 3:
                        if after_total is not None:
                            after_total()
                        dve.wait_ge(gl_sig, 2 * i + 2)
                        own.done(dve.tensor_tensor(hid[:, 1, :, :], hid[:, 0, :, :], hid[:, 1, :, :], ALU.mult))
                        own.need()
                        dve.tensor_tensor(block_, block_, hid[:, 1, :, :], ALU.add).then_inc(m_made, 1)

            def m_lo_of(b):
                blocks = slice(4 * b, 4 * b + 4)
                lo_of(mx[:, blocks, S:2 * S], m32[:, blocks, :], mx[:, blocks, 0:S], b + 1, m_hi, m_lo)

            with dve.Fori(0, 3) as i:
                own.enter(i, 2)
                merge(i, 8 * i + 34, 4 * i + 17)
                own.leave(3)
            merge(3, 58, 29, after_total=lambda: m_lo_of(0))
            for b in range(1, 4):
                m_lo_of(b)
            with dve.Fori(0, 2) as i:
                own.enter(i, 2)
                for k in range(2):
                    blocks = ds(8 * i + 4 * k, 4)
                    plain(4 * i + 2 * k + 66, 2 * i + k + 33, psum[k], zz[:, blocks, :])
                    own.done(dve.scalar_tensor_tensor(zz[:, blocks, :], xx[:, blocks, 0:S].bitcast(F32), ALPHA,
                                                      zz[:, blocks, :], ALU.mult, ALU.add))
                    own.need()
                    dve.scalar_tensor_tensor(zz[:, blocks, :], xx[:, blocks, S:2 * S].bitcast(F32), ALPHA,
                                             zz[:, blocks, :], ALU.mult, ALU.add).then_inc(z_made, 1)
                own.leave(2)

            def each_token(t):
                return t[:, :].unsqueeze(1).to_broadcast([P, SN, S])

            def centre(n, src):
                dve.wait_ge(nmean[n], 1)
                for b in range(4):
                    dve.tensor_tensor(src[:, 4 * b:4 * b + 4, :], src[:, 4 * b:4 * b + 4, :], each_token(mean),
                                      ALU.subtract).then_inc(ncent[n], 1)

            def inverse(n):
                dve.wait_ge(nsd[n], 1)
                own.done(dve.reciprocal(rstd[:, :], sdev[:, :]))

            def normed(n, src, base, gain, shift):
                inverse(n)
                own.need()
                for b in range(5):
                    if b < 4:
                        h = hnorm[:, b % 2, :, :]
                        if b >= 2:
                            dve.wait_ge(xx_lo, base + b - 1)
                        if n == 0 and b >= 2:
                            dve.wait_ge(res_seed, b - 1)
                        own.done(dve.tensor_tensor(h, src[:, 4 * b:4 * b + 4, :], each_token(rstd), ALU.mult))
                        own.need()
                        for j in range(SN):
                            t = 4 * b + j
                            last = dve.tensor_scalar(h[:, j, :], h[:, j, :], column(gain, t),
                                                     column(shift, t) if shift else None, ALU.mult,
                                                     *([ALU.add] if shift else []))
                        last.then_inc(nh[n], 1)
                    if b >= 1:
                        c = b - 1
                        blocks = slice(4 * c, 4 * c + 4)
                        lo_of(xx[:, blocks, S:2 * S], hnorm[:, c % 2, :, :], xx[:, blocks, 0:S],
                              base + c + 1, xx_hi, xx_lo)

            centre(0, zz)
            normed(0, zz, 4, "ln1_g", "ln1_b")
            with dve.Fori(0, 8) as i:
                own.enter(i, 4)
                q, e = 8 * i + 74, 6 * i + 37
                for k in range(2):
                    los(q + 2 * k + 1)
                    los(q + 2 * k + 2)
                    dve.wait_ge(half_out, e + k + 1)
                    for j in range(SN):
                        last = dve.scalar_tensor_tensor(hid[:, k, j, :], psum[k][:, j, 0:S],
                                                        column("b1", 4 * k + j + 8 * i), half[:, j, :], ALU.add, ALU.add)
                    last.then_inc(strip_out, 1)
                    dve.wait_ge(strip_out, outs(e + k + 1))
                    dve.scalar_tensor_tensor(hid[:, k, :, :], hid[:, k, :, :], 0.0, hid[:, k, :, :], ALU.max,
                                             ALU.mult).then_inc(ff_made, 1)
                    lo_of(ff[:, 4 * k:4 * k + 4, S:2 * S], hid[:, k, :, :], ff[:, 4 * k:4 * k + 4, 0:S],
                          2 * i + k + 1, ff_hi, ff_lo)
                dve.wait_ge(res_seed, 4)
                for p in range(0, 4, 2):
                    los(q + p + 5)
                    lo(q + p + 6, 0)
                    add_total(e + 2 + p, GA, res[:, 4 * p:4 * p + 4, :])
                    lo(q + p + 6, 2)
                    add_total(e + 3 + p, GB, res[:, 4 * p + 4:4 * p + 8, :])
                own.leave(8)
            centre(1, res)
            inverse(1)
            own.need()
            def gained_lo(dst, b, base, gain):
                dve.wait_ge(xx_hi, base + b + 1)
                for j in range(SN):
                    t = ds(4 * b + j, 1)
                    last = dve.scalar_tensor_tensor(dst[:, t, S:2 * S], res[:, t, :], column(gain, j + 4 * b),
                                                    dst[:, t, 0:S].bitcast(F32), ALU.mult, ALU.subtract)
                last.then_inc(xx_lo, 1)

            def invert_rms(n):
                dve.wait_ge(nsd[n], 1)
                dve.reciprocal(rms[:, :], rms[:, :]).then_inc(rms_ready, 1)

            for b in range(5):
                if b < 4:
                    h = res[:, 4 * b:4 * b + 4, :]
                    own.done(dve.tensor_tensor(h, h, each_token(rstd), ALU.mult))
                    own.need()
                    for j in range(SN):
                        last = dve.tensor_scalar(h[:, j, :], h[:, j, :], column("ln2_g", 4 * b + j),
                                                 column("ln2_b", 4 * b + j), ALU.mult, ALU.add)
                    last.then_inc(nh[1], 1)
                if b >= 1:
                    gained_lo(xx, b - 1, 8, "n1_g")
            los(139)
            lo(140, 0)
            invert_rms(2)
            lo(140, 2)
            total(85, GA, qkv[:, 0:4, :])
            plain(140, 86, GB, qkv[:, 4:8, :])
            dve.memset(bpad[:, :, :], 0.0).then_inc(bg_sum, 1)
            dve.wait_ge(bg_sum, 1)
            dve.wait_ge(bg_sig, 1)
            own.done(dve.tensor_tensor(bpad[:, :, 30:30 + S], qkv[:, 0:4, :], qkv[:, 4:8, :], ALU.mult))

            def taps2(k0, n):
                steps = [None] * 4
                own.need()
                for m in range(n):
                    for tile in range(4):
                        y, x = bconv[:, tile, :], bpad[:, tile, ds(k0 + m, S)]
                        if m:
                            own.need(steps[tile])
                        ins = dve.scalar_tensor_tensor(y, x, column("cv_w", tile + 4 * (k0 + m)), y, ALU.mult, ALU.add)
                        if isinstance(k0, int) and k0 + m == TAPS2 - 1:
                            ins.then_inc(b_made, 1)
                        else:
                            steps[tile] = own.done(ins)

            lo(143, 0)
            own.need()
            for tile in range(4):
                own.done(dve.tensor_scalar(bconv[:, tile, :], bpad[:, tile, 0:S], column("cv_w", tile),
                                           column("cv_b", tile), ALU.mult, ALU.add))
            with dve.Fori(0, 2) as i:
                own.enter(i, 48)
                for k in range(2):
                    q, e, m = 4 * i + 2 * k + 142, 2 * i + k + 87, 2 * i + k
                    lo(q + 1, 2)
                    taps2(6 * m + 1, 2)
                    lo(q + 2, 0)
                    taps2(6 * m + 3, 2)
                    lo(q + 2, 2)
                    total(e, psum[k], qkv[:, ds(8 + 8 * i + 4 * k, 4), :])
                    lo(q + 3, 0)
                    taps2(6 * m + 5, 2)
                own.leave(2)
            lo(151, 2)
            taps2(25, 3)
            lo(152, 0)
            taps2(28, 3)
            lo(152, 2)
            total(91, GA, qkv[:, 24:28, :])
            los(153)
            total(92, GB, qkv[:, 28:30, :], 2)
            dve.wait_ge(qk_sd, 1)
            flat = "p b n h -> p (b n h)"
            own.done(dve.reciprocal(rn[:, :, :, :].rearrange(flat), ssd[:, :, :, :].rearrange(flat)))
            own.need()
            own.done(dve.tensor_scalar(rq[:, :, :, :].rearrange(flat), rn[:, :, :, :].rearrange(flat), HD ** -0.5, None,
                                       ALU.mult))
            for blk in range(2):
                for at, n, count in ((0, 4, 4), (4, 16, 1)):
                    last = dve.tensor_copy(rn_rows[:, blk, at:at + count, :].rearrange("p n (h d) -> p n h d", h=2),
                                           rn[:, blk, n:n + count, :].unsqueeze(3).to_broadcast([P, count, 2, HD]))
            last.then_inc(rows_ready, 1)
            dve.wait_ge(b_mean, 1)
            dve.tensor_tensor(bconv[:, :, :], bconv[:, :, :], each_token(bmean), ALU.subtract).then_inc(b_cent, 1)
            dve.wait_ge(k_rows, 1)
            for n in range(5):
                tile = 12 + n if n < 4 else 28
                last = dve.scalar_tensor_tensor(qkv[:, tile, :], qkv[:, tile, :], gqk[:, n // 4:n // 4 + 1],
                                                GB[:, n // 2, (n % 2) * S:(n % 2) * S + S], ALU.mult, ALU.mult)
            last.then_inc(k_ready, 1)
            dve.wait_ge(const_in_sem, 16)

            def prepare(n):
                qt, _, _, kind = PAIRS[n]
                idx, b = NORMED.index(qt), n % 3
                dve.wait_ge(score_psum, n + 1)
                if n >= 3:
                    dve.wait_ge(pt_psum, n - 2)
                for hd in range(2):
                    for blk, cols in ((0, slice(0, P)), (1, slice(P, 3 * P))):
                        last = dve.scalar_tensor_tensor(probs[:, b, hd, cols], GA[:, 2 * (n % 2) + hd, cols],
                                                        rq[:, blk, idx, hd:hd + 1], masks[:, kind, cols],
                                                        ALU.mult, ALU.add)
                last.then_inc(score_out, 1)
                dve.wait_ge(score_out, n + 1)
                own.done(dve.reduce_max(peak[:, b, :, 0], probs[:, b, :, 0:P], AX.X))
                own.done(dve.reduce_max(peak[:, b, :, 1], probs[:, b, :, P:3 * P], AX.X))
                own.need()
                if kind == 0:
                    last = dve.tensor_scalar(negm[:, b, :, :], peak[:, b, :, :], -1.0, None, ALU.mult)
                else:
                    for hd in range(2):
                        last = dve.tensor_scalar(negm[:, b, hd, :], peak[:, b, hd, :], column("sinks", n - 4 + 8 * hd),
                                                 -1.0, ALU.max, ALU.mult)
                last.then_inc(peak_ready, 1)

            prepare(0)
            prepare(1)
            for n in range(13):
                if n < 12:
                    b = n % 3
                    dve.wait_ge(exp_done, n + 1)
                    if PAIRS[n][3]:
                        own.done(dve.tensor_tensor(rsum[:, b, :, :], rsum[:, b, :, :], sink[:, b, :, :], ALU.add))
                        own.need()
                    dve.reciprocal(rsum[:, b, :, :], rsum[:, b, :, :]).then_inc(rsum_ready, 1)
                if n < 10:
                    prepare(n + 2)
                if n == 2:
                    dve.wait_ge(b_sd, 1)
                    own.done(dve.reciprocal(bmean[:, :], bsdev[:, :]))
                    own.need()
                    own.done(dve.tensor_tensor(bconv[:, :, :], bconv[:, :, :], each_token(bmean), ALU.mult))
                    own.need()
                if n == 3:
                    for j in range(4):
                        last = dve.tensor_scalar(bconv[:, j, :], bconv[:, j, :], column("cln_g", j), column("cln_b", j),
                                                 ALU.mult, ALU.add)
                    last.then_inc(b_norm, 1)
                if n == 5:
                    lo_of(xx[:, 4:8, S:2 * S], bconv[:, :, :], xx[:, 4:8, 0:S], 1, b_hi, b_lo)
                if n >= 1:
                    lo_of(xx[:, mix_tile(n - 1), S:2 * S], GB[:, 2 + (n - 1) % 2, 0:S], xx[:, mix_tile(n - 1), 0:S],
                          12 + n, xx_hi, xx_lo)
            with dve.Fori(0, 2) as i:
                own.enter(i, 2)
                for k in range(2):
                    q = 4 * i + 2 * k + 153
                    los(q + 1)
                    los(q + 2)
                    add_total(2 * i + k + 93, psum[k], res[:, ds(8 * i + 4 * k, 4), :])
                    gained_lo(x2, 2 * i + k, 24, "n2_g")
                own.leave(2)
            def gate_strip(q, e):
                plain(q, e, GA, hid[:, 0, :, :])

            def up_strip(q, e, n):
                plain(q, e, GB, hid[:, 1, :, :])
                dve.wait_ge(gate_scaled, n + 1)
                dve.tensor_tensor(hid[:, 1, :, :], hid[:, 1, :, :], hid[:, 0, :, :], ALU.mult).then_inc(ff_made, 1)
                lo_of(ff[:, 0:4, S:2 * S], hid[:, 1, :, :], ff[:, 0:4, 0:S], 17 + n, ff_hi, ff_lo)

            def downs(q, e, first, j, more=True):
                if more:
                    lo(q + 1 + j // 2, 2 * (j % 2))
                add_total(e + j, psum[(j + first) % 2], res[:, 4 * j:4 * j + 4, :])

            los(162)
            lo(163, 0)
            invert_rms(3)
            lo(163, 2)
            total(97, GA, hid[:, 0, :, :])
            up_strip(163, 98, 0)
            with dve.Fori(0, 9) as i:
                own.enter(i, 4)
                q, e = 6 * i + 165, 6 * i + 99
                gate_strip(q, e)
                for j in range(4):
                    downs(q + 2, e + 1, 1, j)
                up_strip(q + 4, e + 5, i + 1)
                own.leave(9)
            gate_strip(219, 153)
            plain(221, 154, GB, hid[:, 1, :, :])
            dve.wait_ge(gate_scaled, 11)
            dve.tensor_tensor(hid[:, 1, :, :], hid[:, 1, :, :], hid[:, 0, :, :], ALU.mult).then_inc(ff_made, 1)
            downs(223, 155, 0, 0)
            lo_of(ff[:, 4:8, S:2 * S], hid[:, 1, :, :], ff[:, 4:8, 0:S], 27, ff_hi, ff_lo)
            for j in range(1, 4):
                downs(223, 155, 0, j)
            for j in range(4):
                downs(225, 159, 0, j, j < 2)

        @block.gpsimd
        def _(pool):
            def lo(q, r, width=N8):
                pool.wait_ge(hi_done, 4 * q + r + 1)
                if not (isinstance(q, int) and q == 0):
                    pool.wait_ge(pe_piece, 4 * q + r - 3)
                pool.tensor_tensor(w_lo[:, r, 0:width], w_raw[:, r, 0:width], w_hi[:, r, 0:width].bitcast(F32),
                                   ALU.subtract).then_inc(lo_pool, 1)

            def los(q, width=N8, slots=(1, 3)):
                for r in slots:
                    lo(q, r, width)

            for q in range(4):
                los(q)
            los(4, N10)

            def three(s, q, wide):
                def times_u(heads):
                    for way in range(2):
                        last = pool.tensor_tensor(gates[:, heads, way, 1, :], gates[:, heads, way, 1, :],
                                                  uf[:, heads, :], ALU.mult)
                    last.then_inc(iu_ready, 1)

                los(q + 1, N10)
                pool.wait_ge(gate_out, 8 * s - 4)
                times_u(slice(0, 2))
                los(q + 2)
                pool.wait_ge(gate_out, 8 * s)
                times_u(slice(2, 4))
                los(q + 3)
                pool.wait_ge(a_ready, s)
                for way in range(2):
                    if way == 0:
                        pool.wait_ge(tanh_ready, s)
                    last = pool.tensor_tensor(gates[:, :, way, 0, :], aa[:, way, :, :], aa[:, way, :, :], ALU.mult)
                last.then_inc(sq_ready, 1)
                los(q + 4)
                los(q + 5)
                los(q + 6, wide)

            with pool.Fori(0, 4) as i:
                three(i + 1, 6 * i + 4, N10)
            three(5, 28, N8)
            with pool.Fori(0, 4) as i:
                for k, width in enumerate((N8, N10, N10, N8, N8, N8, N8, N8)):
                    los(8 * i + 35 + k, width)
            with pool.Fori(0, 8) as i:
                los(i + 67)
            for b in range(4):
                pool.wait_ge(nh[0], b + 1)
                for j in range(SN):
                    t = 4 * b + j
                    last = pool.tensor_scalar(res[:, t, :], hnorm[:, b % 2, j, :], ALPHA,
                                              prm[:, COL["b2"] + t:COL["b2"] + t + 1], ALU.mult, ALU.add)
                last.then_inc(res_seed, 1)
            with pool.Fori(0, 64) as i:
                los(i + 75)

            def sum_squares(n):
                for b in range(1, 4):
                    pool.wait_ge(nsq[n], b + 1)
                    if b >= 2:
                        pool.wait_ge(pool_step, 2 * (n - 2) + b - 1)
                    pool.tensor_tensor(squares[:, 0:4, :], squares[:, 0:4, :], squares[:, 4 * b:4 * b + 4, :],
                                       ALU.add).then_inc(pool_step if b < 3 else sq_summed, 1)


            sum_squares(2)

            def by_token(t):
                return rms[:, :].unsqueeze(1).to_broadcast([P, t, S])

            def scale_strip(e, tiles, n=SN):
                pool.wait_ge(strip_out, outs(e + 1))
                pool.wait_ge(rms_ready, 1)
                pool.tensor_tensor(tiles, tiles, by_token(n), ALU.mult).then_inc(qkv_made, 1)

            with pool.Fori(0, 7) as i:
                los(2 * i + 139)
                los(2 * i + 140)
                scale_strip(i + 85, qkv[:, ds(4 * i, 4), :])
            los(153)
            scale_strip(92, qkv[:, 28:30, :], 2)
            for n in range(12):
                b = n % 3
                pool.wait_ge(rsum_ready, n + 1)
                for hd in range(2):
                    for blk, cols in ((0, slice(0, P)), (1, slice(P, 3 * P))):
                        last = pool.tensor_scalar(probs[:, b, hd, cols], probs[:, b, hd, cols],
                                                  rsum[:, b, hd, blk:blk + 1], None, ALU.mult)
                last.then_inc(p_ready, 1)
            with pool.Fori(0, 8) as i:
                los(i + 154)

            def scale_gate(signal):
                pool.tensor_tensor(hid[:, 0, :, :], hid[:, 0, :, :], by_token(SN), ALU.mult).then_inc(signal, 1)

            def gate_strip(q, e, n):
                los(q + 1)
                los(q + 2)
                pool.wait_ge(strip_out, outs(e + 1))
                pool.wait_ge(rms_ready, 2)
                scale_gate(gate_sum)
                los(q + 3)
                pool.wait_ge(gate_act, n + 1)
                scale_gate(gate_scaled)
                los(q + 4)

            sum_squares(3)
            gate_strip(161, 97, 0)
            with pool.Fori(0, 9) as i:
                gate_strip(6 * i + 165, 6 * i + 99, i + 1)
                los(6 * i + 170)
                los(6 * i + 171)
            gate_strip(219, 153, 10)
            for q in range(224, 227):
                los(q)


def mix_tile(n):
    return n if n < 4 else n + 4


def strips(w, width=SN * P, per=2):
    rows, cols = w.shape
    a = w.reshape(rows // (per * P), per, P, cols // width, width)
    return a.transpose(3, 0, 2, 1, 4).reshape(-1, P, per * width)


def tiles_of(w):
    rows, cols = w.shape
    return w.reshape(rows // P, P, cols // P, P).transpose(0, 2, 1, 3).reshape(-1, P, P)


def pieces10(tiles):
    return tiles.reshape(-1, 10, P, P).transpose(0, 2, 1, 3).reshape(-1, P, N10)


def columns(v):
    v = np.asarray(v).reshape(-1, P)
    return v.T


def lay_out(a):
    edges = np.cumsum([0, LRU_W, CONV_W, CONV_W, CONV_W, D, D])
    w = a["w_in"]
    w_lru, w_x, w_b, w_c, w_gl, w_gc = (w[:, edges[k]:edges[k + 1]] for k in range(6))
    strip = lambda m, s: m[:, SN * P * s:SN * P * (s + 1)]
    s8 = [strips(strip(w_lru, 0)), strips(strip(w_b, 3))]
    s10 = []
    for s in range(1, 6):
        main = tiles_of(strip(w_lru, s) if s < 5 else strip(w_b, 0)).reshape(8, 8, P, P)
        heads = slice(4 * (s - 1), 4 * s)
        gate_tiles = np.stack([a["lru_w_a"][:, heads], a["lru_w_x"][:, heads]], 2)
        pairs = gate_tiles.transpose(1, 0, 2, 3, 4).reshape(8, 2, P, P)
        s10.append(pieces10(np.concatenate([main, pairs], 1).reshape(-1, P, P)))
    for s in range(4):
        s8 += [strips(strip(w_x, s)), strips(strip(w_c, s))]
    s8 += [strips(strip(w_b, s)) for s in range(1, 3)]
    for s in range(4):
        s8 += [strips(strip(w_gl, s)), strips(strip(w_gc, s)), strips(strip(a["w_conv_out"], s))]
        s10.append(pieces10(tiles_of(strip(a["w_lru_out"], s))))
    s8.append(strips(a["w_o"]))
    for i in range(8):
        rows = slice(8 * P * i, 8 * P * (i + 1))
        turns = strips(a["mlp_w2"][rows]).reshape(2, 2, 2, 2, P, N8).transpose(0, 2, 1, 3, 4, 5).reshape(-1, P, N8)
        s8 += [strips(a["mlp_w1"][:, rows]), turns]
    w2 = a["w_in_2"][0]
    at = np.cumsum([0, 512, 512, 512, 512, 512, 1024, 128, 128])
    aq, ak, av, bu, bg, cq, ck, cv = (w2[:, at[k]:at[k + 1]] for k in range(8))
    cq = cq.reshape(D, 2, 8, HD).transpose(0, 2, 1, 3).reshape(D, C_HEADS * HD)
    s8.append(strips(np.concatenate([bu, bg, aq, ak, av, cq], 1)))
    s8.append(strips(np.concatenate([ck, cv], 1), 2 * P, 4))
    wo = a["w_out_2"][0]
    woc = wo[D // 2:].reshape(2, 8, HD, D).transpose(1, 0, 2, 3).reshape(D // 2, D)
    s8.append(strips(np.concatenate([wo[:D // 2], woc])))
    n2 = D_FF2 // (SN * P)
    gate, up = a["w_gate_2"][0], a["w_up_2"][0]
    down = lambda s: strips(a["w_down_2"][0][SN * P * s:SN * P * (s + 1)])
    s8 += [strips(strip(gate, 0)), strips(strip(up, 0))]
    for s in range(1, n2 - 1):
        s8 += [strips(strip(gate, s)), down(s - 1), strips(strip(up, s))]
    s8 += [strips(strip(gate, n2 - 1)), strips(strip(up, n2 - 1)), down(n2 - 2), down(n2 - 1)]
    twice = lambda g: np.concatenate([g[0], g[0]])
    values = dict(
        lru_w=a["lru_conv_w"], lru_b=a["lru_conv_b"], b_a=a["lru_b_a"], b_x=a["lru_b_x"], lam=a["lru_lambda"],
        sc_w=a["sc_conv_w"], sc_b=a["sc_conv_b"], ln1_g=a["ln1_g"], ln1_b=a["ln1_b"], b1=a["mlp_b1"], b2=a["mlp_b2"],
        ln2_g=a["ln2_g"], ln2_b=a["ln2_b"], n1_g=a["norm1_g_2"], aq_g=twice(a["a_q_g_2"]), ak_g=twice(a["a_k_g_2"]),
        cq_g=twice(a["c_q_g_2"]), ck_g=twice(a["c_k_g_2"]), cv_w=a["conv_w_2"][0], cv_b=a["conv_b_2"],
        cln_g=a["conv_ln_g_2"], cln_b=a["conv_ln_b_2"], n2_g=a["norm2_g_2"],
        sinks=np.repeat(a["c_sinks_2"][0], P))
    prm = np.concatenate([columns(values[name]) for name, _ in PARAM_SIZES], 1)
    x = a["x"][0].T.reshape(KT, P, S).transpose(1, 0, 2)
    return dict(x=x, prm=prm, const=constants(), w8=np.concatenate(s8), w10=np.concatenate(s10))


def constants():
    q, k = np.arange(S)[:, None], np.arange(S)[None, :]
    dist = q - k
    reached = sum(((dist >= 0) & (dist <= w) & (dist % d == 0)).astype(int)
                  for w, d in ((128, 1), (512, 4), (2048, 16)))
    mask_a = np.where(reached > 0, np.log(np.maximum(reached, 1)), -1e30)
    mask_c = np.where((dist >= 0) & (dist < 128), 0.0, -1e30)
    blocks = [np.concatenate([m[:P, :P], m[P:, :P], m[P:, P:]], 1) for m in (mask_a, mask_c)]
    halves = (np.arange(P)[:, None] // HD == np.arange(2)[None, :]).astype(float)
    return np.concatenate([np.eye(P), *blocks, halves], 1).astype(np.float32)


def kernel(**inputs):
    import concourse.bacc as bacc
    from concourse.bass_utils import run_bass_kernel_spmd

    arrays = {k: np.ascontiguousarray(v) for k, v in lay_out({k: np.asarray(v) for k, v in inputs.items()}).items()}
    nc = bacc.Bacc("TRN2", target_bir_lowering=False, num_devices=1)
    aps = [nc.dram_tensor(f"{k}_dram", arrays[k].shape, F32, kind="ExternalInput").ap()
           for k in ("x", "prm", "const", "w8", "w10")]
    out = nc.dram_tensor("out_dram", (P, KT, S), F32, kind="ExternalOutput").ap()
    build(nc, *aps, out)
    got = run_bass_kernel_spmd(nc, [{f"{k}_dram": v for k, v in arrays.items()}], core_ids=[0])
    y = got.results[0]["out_dram"]
    return np.ascontiguousarray(y.transpose(2, 1, 0)).reshape(1, S, D)
```
